# Optimizing a Trainium2 kernel written in Bass

```python
import jax, jax.numpy as jnp
from jax import lax
import numpy as np

D_MODEL = 1024
BATCH = 1
SEQ = 512
DEPTH = 1
DEC_BATCH = 8
DEC_SEQ = 8
PAST_LEN = 1024
PAGE_SIZE = 128

N_HEADS = 16
N_KV_HEADS = 4
HEAD_DIM = D_MODEL // N_HEADS
GROUP = N_HEADS // N_KV_HEADS
WINDOW = 128
ATTN_BLOCK = WINDOW
D_ATTN = N_HEADS * HEAD_DIM
D_KV = N_KV_HEADS * HEAD_DIM
REC_HEADS = 8
REC_DK = 128
REC_DV = D_MODEL // REC_HEADS
D_REC_K = REC_HEADS * REC_DK
D_REC_V = REC_HEADS * REC_DV
REC_CHUNK = 64
D_FF = 4 * D_MODEL
N_MOD = 6
EPS = 1e-6
MASK_VALUE = -1e30
IN_SIZES = (D_ATTN, D_KV, D_KV, D_REC_K, D_REC_K, D_REC_V, D_REC_V, D_MODEL, D_MODEL)
IN_COLS = sum(IN_SIZES)

kernel_name = 'hybrid_swa_sink_alibi_hgrn2_adaln_step'

def rms_norm(x, g):
    xf = x.astype(jnp.float32)
    y = xf * lax.rsqrt(jnp.mean(jnp.square(xf), axis=-1, keepdims=True) + EPS)
    return (y * g.astype(jnp.float32)).astype(x.dtype)

def alibi_slopes():
    return 2.0 ** (-8.0 * jnp.arange(1, N_HEADS + 1, dtype=jnp.float32) / N_HEADS)

def sink_attention(q, k, v, qpos, kpos, sinks):
    s = jnp.einsum('bnqkgd,bnskd->bnkgqs', q, k).astype(jnp.float32) * HEAD_DIM ** -0.5
    dist = qpos[:, :, None] - kpos[:, None, :]
    valid = (dist >= 0) & (dist <= WINDOW) & (kpos[:, None, :] >= 0)
    slopes = alibi_slopes().reshape(N_KV_HEADS, GROUP)[None, None, :, :, None, None]
    s = s - slopes * dist.astype(jnp.float32)[None, :, None, None]
    s = jnp.where(valid[None, :, None, None], s, MASK_VALUE)
    sink = sinks.astype(jnp.float32).reshape(N_KV_HEADS, GROUP)[None, None, :, :, None, None]
    m = jnp.maximum(jnp.max(s, axis=-1, keepdims=True), sink)
    p = jnp.exp(s - m)
    p = p / (jnp.sum(p, axis=-1, keepdims=True) + jnp.exp(sink - m))
    return jnp.einsum('bnkgqs,bnskd->bnqkgd', p.astype(v.dtype), v)

def swa_prompt(q, k, v, sinks):
    B, L = q.shape[:2]
    nb = L // ATTN_BLOCK
    qb = q.reshape(B, nb, ATTN_BLOCK, N_KV_HEADS, GROUP, HEAD_DIM)

    def with_prev(t):
        t = t.reshape(B, nb, ATTN_BLOCK, N_KV_HEADS, HEAD_DIM)
        prev = jnp.concatenate([jnp.zeros_like(t[:, :1]), t[:, :-1]], axis=1)
        return jnp.concatenate([prev, t], axis=2)

    start = jnp.arange(nb) * ATTN_BLOCK
    qpos = start[:, None] + jnp.arange(ATTN_BLOCK)[None]
    kpos = start[:, None] - ATTN_BLOCK + jnp.arange(2 * ATTN_BLOCK)[None]
    o = sink_attention(qb, with_prev(k), with_prev(v), qpos, kpos, sinks)
    return o.reshape(B, L, D_ATTN)

def swa_sample(q, k, v, buf_k, buf_v, sinks):
    B, L = q.shape[:2]
    w = buf_k.shape[1]
    k_all = jnp.concatenate([buf_k, k.astype(buf_k.dtype)], axis=1)
    v_all = jnp.concatenate([buf_v, v.astype(buf_v.dtype)], axis=1)
    qpos = (PAST_LEN + jnp.arange(L))[None]
    kpos = (PAST_LEN - w + jnp.arange(w + L))[None]
    o = sink_attention(q.reshape(B, 1, L, N_KV_HEADS, GROUP, HEAD_DIM),
                       k_all[:, None], v_all[:, None], qpos, kpos, sinks)
    return o.reshape(B, L, D_ATTN), k_all[:, -w:], v_all[:, -w:]

def hgrn2_chunked(q, k, v, logf, s0):
    B, L, H, _ = q.shape
    C = min(REC_CHUNK, L)
    n = -(-L // C)
    pad = n * C - L

    def prep(t):
        t = jnp.pad(t, ((0, 0), (0, pad), (0, 0), (0, 0)))
        return jnp.moveaxis(t.reshape(B, n, C, H, t.shape[-1]), 1, 0)

    tri = jnp.tril(jnp.ones((C, C), dtype=bool))[None, :, :, None, None]

    def step(S, inp):
        qc, kc, vc, gc = inp
        b = jnp.cumsum(gc, axis=1)
        o_inter = jnp.einsum('bthk,bhkv->bthv', qc * jnp.exp(b), S)
        diff = b[:, :, None] - b[:, None, :]
        decay = jnp.where(tri, jnp.exp(jnp.where(tri, diff, 0.0)), 0.0)
        att = jnp.einsum('bthk,bshk,btshk->bhts', qc, kc, decay)
        o_intra = jnp.einsum('bhts,bshv->bthv', att, vc)
        b_last = b[:, -1]
        S = jnp.exp(b_last)[..., None] * S + jnp.einsum(
            'bshk,bshv->bhkv', kc * jnp.exp(b_last[:, None] - b), vc)
        return S, o_inter + o_intra

    S, o = lax.scan(step, s0, (prep(q), prep(k), prep(v), prep(logf)))
    o = jnp.moveaxis(o, 0, 1).reshape(B, n * C, H, v.shape[-1])[:, :L]
    return o, S

def layer(x, c, prm, lb, s0, w_buf, buf_k=None, buf_v=None):
    (norm_mix, norm_mlp, w_ada, b_ada, w_in, sinks, hgrn_norm, w_out, w_up, w_down) = prm
    B, L, _ = x.shape
    mod = (jax.nn.silu(c) @ w_ada + b_ada)[:, None, :]
    sh_a, sc_a, g_a, sh_m, sc_m, g_m = jnp.split(mod, N_MOD, axis=-1)

    h = rms_norm(x, norm_mix) * (1.0 + sc_a) + sh_a
    z = h @ w_in
    q, k, v, rq, rf, ri, rg, ga, gr = jnp.split(
        z, np.cumsum(IN_SIZES)[:-1].tolist(), axis=-1)

    q = q.reshape(B, L, N_HEADS, HEAD_DIM)
    k = k.reshape(B, L, N_KV_HEADS, HEAD_DIM)
    v = v.reshape(B, L, N_KV_HEADS, HEAD_DIM)
    if buf_k is None:
        o_attn = swa_prompt(q, k, v, sinks)
        new_k, new_v = k[:, -w_buf:], v[:, -w_buf:]
    else:
        o_attn, new_k, new_v = swa_sample(q, k, v, buf_k, buf_v, sinks)

    fp = rf.astype(jnp.float32).reshape(B, L, REC_HEADS, REC_DK)
    lbh = lb.reshape(REC_HEADS, REC_DK)
    sig = jax.nn.sigmoid(fp)
    logf = jnp.log(lbh + (1.0 - lbh) * sig)
    kr = (1.0 - lbh) * (1.0 - sig)
    qr = jax.nn.silu(rq.astype(jnp.float32)).reshape(B, L, REC_HEADS, REC_DK) * REC_DK ** -0.5
    vr = ri.astype(jnp.float32).reshape(B, L, REC_HEADS, REC_DV)
    o_rec, s_new = hgrn2_chunked(qr, kr, vr, logf, s0.astype(jnp.float32))
    o_rec = rms_norm(o_rec, hgrn_norm.reshape(REC_HEADS, REC_DV)) * jax.nn.silu(
        rg.astype(jnp.float32).reshape(B, L, REC_HEADS, REC_DV))
    o_rec = o_rec.reshape(B, L, D_REC_V).astype(x.dtype)

    mixed = jax.nn.sigmoid(ga) * o_attn + jax.nn.sigmoid(gr) * o_rec
    x = x + g_a * (mixed @ w_out)

    h2 = rms_norm(x, norm_mlp) * (1.0 + sc_m) + sh_m
    x = x + g_m * (jnp.square(jax.nn.relu(h2 @ w_up)) @ w_down)
    return x, new_k, new_v, s_new.astype(s0.dtype)

def setup_inputs(seed: int = 0) -> dict:
    key = jax.random.key(seed)
    ks = jax.random.split(key, 22)
    w_buf = min(WINDOW, PAST_LEN)

    def nrm(k, shape, scale):
        return jax.random.normal(k, shape, jnp.float32) * scale

    return {
        'x_prompt': nrm(ks[0], (BATCH, SEQ, D_MODEL), 1.0),
        'x_sample': nrm(ks[1], (DEC_BATCH, DEC_SEQ, D_MODEL), 1.0),
        'cache_win_k': nrm(ks[2], (DEPTH, DEC_BATCH, w_buf, N_KV_HEADS, HEAD_DIM), 1.0),
        'cache_win_v': nrm(ks[3], (DEPTH, DEC_BATCH, w_buf, N_KV_HEADS, HEAD_DIM), 1.0),
        'state_hgrn': nrm(ks[4], (DEPTH, DEC_BATCH, REC_HEADS, REC_DK, REC_DV), 0.3),
        'c_prompt': nrm(ks[5], (BATCH, D_MODEL), 1.0),
        'c_sample': nrm(ks[6], (DEC_BATCH, D_MODEL), 1.0),
        'norm_mix': 1.0 + nrm(ks[7], (DEPTH, D_MODEL), 0.02),
        'norm_mlp': 1.0 + nrm(ks[8], (DEPTH, D_MODEL), 0.02),
        'w_ada': nrm(ks[9], (DEPTH, D_MODEL, N_MOD * D_MODEL), 0.5 * D_MODEL ** -0.5),
        'b_ada': nrm(ks[10], (DEPTH, N_MOD * D_MODEL), 0.02),
        'w_in': nrm(ks[11], (DEPTH, D_MODEL, IN_COLS), D_MODEL ** -0.5),
        'attn_sinks': nrm(ks[12], (DEPTH, N_HEADS), 0.5),
        'hgrn_lb_logits': nrm(ks[13], (DEPTH, D_REC_K), 0.5),
        'hgrn_norm': 1.0 + nrm(ks[14], (DEPTH, D_REC_V), 0.02),
        'w_out': nrm(ks[15], (DEPTH, D_MODEL, D_MODEL), D_MODEL ** -0.5),
        'w_up': nrm(ks[16], (DEPTH, D_MODEL, D_FF), D_MODEL ** -0.5),
        'w_down': nrm(ks[17], (DEPTH, D_FF, D_MODEL), D_FF ** -0.5),
        'final_norm': 1.0 + nrm(ks[18], (D_MODEL,), 0.02),
    }

def reference(x_prompt, x_sample, cache_win_k, cache_win_v, state_hgrn, c_prompt, c_sample,
              norm_mix, norm_mlp, w_ada, b_ada, w_in, attn_sinks, hgrn_lb_logits, hgrn_norm,
              w_out, w_up, w_down, final_norm):
    w_buf = cache_win_k.shape[2]
    p_lb = jax.nn.softmax(hgrn_lb_logits.astype(jnp.float32), axis=0)
    lb_all = jnp.cumsum(p_lb, axis=0) - p_lb[0]

    xp, xs = x_prompt, x_sample
    pk, pv, ps, sk, sv, ss = [], [], [], [], [], []
    for l in range(DEPTH):
        prm = (norm_mix[l], norm_mlp[l], w_ada[l], b_ada[l], w_in[l], attn_sinks[l],
               hgrn_norm[l], w_out[l], w_up[l], w_down[l])
        s0p = jnp.zeros((xp.shape[0], REC_HEADS, REC_DK, REC_DV), xp.dtype)
        xp, k_p, v_p, s_p = layer(xp, c_prompt, prm, lb_all[l], s0p, w_buf)
        xs, k_s, v_s, s_s = layer(xs, c_sample, prm, lb_all[l], state_hgrn[l], w_buf,
                                  cache_win_k[l], cache_win_v[l])
        pk.append(k_p); pv.append(v_p); ps.append(s_p)
        sk.append(k_s); sv.append(v_s); ss.append(s_s)

    y_prompt = rms_norm(xp, final_norm)
    y_sample = rms_norm(xs, final_norm)
    return (y_prompt, y_sample, jnp.stack(pk), jnp.stack(pv), jnp.stack(ps),
            jnp.stack(sk), jnp.stack(sv), jnp.stack(ss))


_drawn_inputs = setup_inputs


def setup_inputs(seed=0):
    import zlib

    import numpy as np

    out = dict(_drawn_inputs(seed))
    spreads = {}
    factors = {'state_hgrn': 8.0,
     'norm_mix': 2.82,
     'norm_mlp': 6.358,
     'attn_sinks': 29.853,
     'hgrn_norm': 8.0,
     'final_norm': 8.563}
    for name, (base, spread) in spreads.items():
        noise = np.random.default_rng([zlib.crc32(name.encode()), seed]).standard_normal(out[name].shape)
        drawn = base * np.exp(spread * noise) if base else spread * noise
        out[name] = __import__('jax').numpy.asarray(drawn.astype(out[name].dtype))
    for name, factor in factors.items():
        out[name] = (out[name] * factor).astype(out[name].dtype)
    return out
```

```python
import concourse.bass as bass
from concourse import mybir
from contextlib import ExitStack

F32 = mybir.dt.float32
F32R = mybir.dt.float32r
U8 = mybir.dt.uint8
ALU = mybir.AluOpType
ACT = mybir.ActivationFunctionType
AX = mybir.AxisListType

P = 128
DM = 1024
KT = DM // P
SEQ = 512
NB, NT = 8, 8
SMP = NB * NT
TOK = SEQ + SMP
HALF = TOK // 2
TT = SEQ // P
HEADS, KV, HD = 16, 4, 64
GRP = HEADS // KV
WIN = 128
RH = 8
DFF = 4 * DM
EPS = 1e-6
UC = 256
UW = KT * UC
NSEQ = 1 + NB
SEG = dict(q=0, k=1024, v=1280, rq=1536, rf=2560, ri=3584, rg=4608, ga=5632, gr=6656)
LEVELS = (64, 32, 16, 8, 4, 2, 1)
NL = len(LEVELS)
QSCALE = 0.5 * P ** -0.5
LEAST = 1e-19
VN = dict(mix=0, mlp=8, hgrn=16, fin=24, lb=32, bada=40)
NVEC = 88


def units():
    w_in = [("k", 0), ("v", 0)] + [("q", i) for i in range(4)]
    for p in (0, 1):
        w_in += [("rf", p), ("rq", p), ("ri", p)]
    w_in += [("ga", i) for i in range(4)]
    for p in (2, 3):
        w_in += [("rf", p), ("rq", p), ("ri", p)]
    for p in range(4):
        w_in += [("gr", p), ("rg", p)]
    out = [("ada", i) for i in range(8)]
    rest = [("ada", i) for i in range(8, 20)]
    for u in w_in:
        out.append(u)
        if rest:
            out.append(rest.pop(0))
    out += [("out", i) for i in range(4)]
    out += [("ada", i) for i in range(20, 24)]
    out += [("up", 0), ("up", 1)]
    for g in range(1, 8):
        out += [("up", 2 * g), ("up", 2 * g + 1), ("dn", 2 * g - 2), ("dn", 2 * g - 1)]
    return out + [("dn", 14), ("dn", 15)]


UNITS = units()
NTILES = dict(ada=1, v=5, ri=5, dn=4)
READER = dict(ada="dve", k="act", v="act", q="act", rf="act", ri="act", ga="act", gr="act", up="act",
              rq="tanh", rg="tanh", out="dve", dn="dve")
CHUNKS = dict(ada=1, v=2, ri=2, dn=2)


FRONT = 8
LATE = [u for u, x in enumerate(UNITS) if x[0] == "ada" and x[1] >= 20]
RING = [u for u in range(FRONT, len(UNITS)) if u not in LATE]
SLOT = {u: n % 2 for n, u in enumerate(RING)}
BEFORE = {u: RING[n - 2] for n, u in enumerate(RING) if n >= 2}
AFTER = {u: RING[n + 2] for n, u in enumerate(RING) if n + 2 < len(RING)}
JOINT = (("k", 0), ("up", 0))


class Tile:

    def __init__(self, t, u, kind, i, n, split):
        self.t, self.u, self.kind, self.i, self.n, self.split = t, u, kind, i, n, split
        self.pair = t % 2


def tiles():
    out, split = [], 0
    for u, (kind, i) in enumerate(UNITS):
        for n in range(NTILES.get(kind, 2)):
            out.append(Tile(len(out), u, kind, i, n, split))
        split += kind != "ada"
    return out


TILES = tiles()
SPLITS = [u for u, (kind, _) in enumerate(UNITS) if kind != "ada"]
LAST = {u: max(x.t for x in TILES if x.u == u) for u in range(len(UNITS))}
TANH = [x.t for x in TILES if x.kind in ("rq", "ga", "gr", "rg")]


def count_read(t, reader):
    if reader == "tanh":
        return TANH.index(t) + 1
    return sum(READER[x.kind] == reader for x in TILES[:t + 1])


PREP, SAMP = 4, 4 + NB
STEPS = SAMP + (HEADS // 2) * TT


def prep_slots():
    for s in range(PREP):
        yield [("a_score", s), ("a_max", s)]


def attention_slots():
    for s in range(PREP, STEPS + 3):
        ev = []
        if s >= PREP + 3:
            ev += [("a_turn", s - 3), ("a_put", s - 3)]
        if PREP + 2 <= s < STEPS + 2:
            ev += [("a_value", s - 2), ("a_scale", s - 2)]
        if PREP + 1 <= s < STEPS + 1:
            ev += [("a_probs", s - 1), ("a_take", s - 1)]
        if s < STEPS:
            ev = [("a_score", s)] + ev + [("a_max", s), ("a_exp", s)]
        yield ev
    yield [("win", 0)]


def hgrn_slots(pair):
    def begin(r):
        return [("g_start", r), ("g_diff", r, 0), ("g_diff", r, 1), ("g_exp", r, 0), ("g_diff", r, 2), ("g_operands", r, 0), ("g_exp", r, 1)]

    yield begin(2 * pair)
    for r in (2 * pair, 2 * pair + 1):
        for k in range(NL + 2):
            ev = []
            if k == 0:
                ev += [("g_diag", r)]
            if k < NL:
                if k + 1 < NL:
                    ev += [("g_operands", r, k + 1)]
                ev += [("g_level", r, k)]
                if k + 2 < NL:
                    ev += [("g_exp", r, k + 2)]
                if k + 3 < NL:
                    ev += [("g_diff", r, k + 3)]
            if k == 1:
                ev += [("g_hats", r)]
            if k == 2:
                ev += [("g_keys", r)]
            if k == 3:
                ev += [("g_state", r)]
            if k in (4, 5):
                ev += [("g_sample", r, k - 4)]
            if k == NL:
                ev += [("g_out", r)]
                if r % 2 == 0:
                    ev += begin(r + 1)
            if k == NL + 1:
                ev += [("g_norm", r)]
            yield ev


def walk():
    first = {}
    for x in TILES:
        first.setdefault((x.kind, x.i), x.t)
    work = [[prep_slots(), first["v", 0], first["rf", 0]],
            [attention_slots(), first["rf", 0], first["ga", 0]],
            [hgrn_slots(0), first["ga", 0], first["rf", 2]],
            [hgrn_slots(1), first["ga", 0], first["rf", 3]],
            [hgrn_slots(2), first["rf", 3], first["gr", 0]],
            [hgrn_slots(3), first["gr", 0], first["gr", 2]]]

    def slot(t):
        while work and work[0][1] <= t:
            ev = next(work[0][0], None)
            if ev is not None:
                return ev
            work.pop(0)
        return []

    yield ("front",)
    for x in TILES:
        while work and work[0][2] <= x.t:
            for ev in work.pop(0)[0]:
                yield from ev
        if x.kind == "k" and x.n == 0:
            yield ("norm", 0)
            yield ("hi", 0)
            for q in range(4):
                yield ("lo", 0, q)
            yield ("load", AFTER[SPLITS[0]])
            yield ("modulate", 0)
        if x.kind == "ada" and x.i == 21:
            yield ("finish_stats", 1)
        if x.kind == "up" and x.i == 0 and x.n == 0:
            yield ("modulate", 1)
        for c in range(CHUNKS.get(x.kind, 4)):
            yield ("mm", x, c)
            at = x.n * CHUNKS.get(x.kind, 4) + c
            if at < 4 and x.kind != "ada" and x.split + 1 < len(SPLITS):
                if at == 0:
                    yield ("hi", x.split + 1)
                yield ("lo", x.split + 1, at)
                if at == 3 and SPLITS[x.split + 1] in AFTER:
                    yield ("load", AFTER[SPLITS[x.split + 1]])
            yield from slot(x.t)
        yield ("evac", x)
        if x.kind == "ada" and x.u in AFTER:
            yield ("load", AFTER[x.u])
        if x.kind == "q" and x.t == LAST[x.u] and x.i == 3:
            yield ("q_blocks",)
        if x.kind == "out":
            yield ("stats", 1, 2 * x.i + x.n)
        if x.kind == "dn" and x.i >= 14:
            yield ("stats", 2, 4 * (x.i - 14) + x.n)
    yield ("finish_stats", 2)
    yield ("final",)


def program(nc, a, o):
    w_in, w_ada = a["w_in"][0], a["w_ada"][0]
    spill = nc.dram_tensor("residual", [P, KT * TOK], F32).ap()

    ctx = ExitStack()
    with ctx:
        def sb(name, shape, dt=F32, stack=ctx):
            return stack.enter_context(nc.sbuf_tensor(name, shape, dt))

        def sem(name):
            return ctx.enter_context(nc.semaphore(name))

        ident = sb("ident", [P, P])
        ones = sb("ones", [P, P])
        levels = sb("levels", [P, NL, HALF], U8)
        resets = sb("resets", [P, TOK], U8)
        own_seq = sb("own_seq", [SMP, NB])
        vec = sb("vec", [P, NVEC])
        mods = sb("mods", [P, 6 * KT, NSEQ])
        cT = sb("cT", [P, KT, NSEQ])
        sink = sb("sink", [P, HEADS])
        sink_s = sb("sink_s", [P, 1])
        eps = sb("eps", [P, 1])
        lb = sb("lb", [P, KT])
        omlb = sb("omlb", [P, KT])
        nomlb = sb("nomlb", [P, KT])
        small = sb("small", [P, 4, 6, 2])
        tmp_s = sb("tmp_s", [P, SMP])
        warm = sb("warm", [P, 1])
        rb = sb("rb", [P, TOK])
        tmp = [sb(f"tmp{i}", [P, TOK]) for i in range(4)]
        hR = sb("hR", [P, 2, KT * TOK + SMP], F32R)
        raw = [sb(f"raw{i}", [P, UW]) for i in range(2)]
        wR = [sb(f"wR{i}", [P, 2, UW], F32R) for i in range(2)]
        xT = sb("xT", [P, KT, TOK])
        attnT = xT

        def stage(*tensors):
            st, out = ExitStack(), []
            for name, shape in tensors:
                out.append(sb(name, shape, F32, st))
            st.close()
            return out

        ZS = [2 * TOK, 2 * TOK, 2 * TOK, 5 * UC]
        (xn, cn, cgate, vrow, *ada) = stage(
            ("xn", [P, TT + 1, DM]), ("cn", [NSEQ, DM]), ("cgate", [NSEQ, DM]), ("vrow", [NVEC, P]),
            *[(f"ada{i}", [P, UW]) for i in range(FRONT)])
        levels_f, resets_f = raw[1][:, 0:NL * HALF], tmp[1]
        (Kc, _, KcT, Qblk, _, Vc, biasP, dist, pr0, pr1, probsT, qT, kT, V, biasS, osb, ) = stage(
            ("Kc", [P, NB, KV * HD]), ("gap0", [P, sum(ZS) - NB * KV * HD]),
            ("KcT", [P, NB, 2, P]), ("Qblk", [P, 2, NB, P]), ("gap1", [P, sum(ZS) - 4 * NB * P]),
            ("Vc", [P, NB, KV * HD]), ("biasP", [P, 2, 2 * P]), ("dist", [P, 2, 2 * P]),
            ("pr0", [P, 512]), ("pr1", [P, 512]), ("probsT", [P, 512]),
            ("qT", [P, KT, TOK]), ("kT", [P, 2, TOK]), ("V", [P, TT + 1, KV * HD]), ("biasS", [P, P + 120]),
            ("osb", [P, P]))
        probs = [pr0, pr1]
        g_names = []
        for s in range(2):
            g_names += [(f"b{s}", [P, 2, TOK]), (f"kr{s}", [P, 2, TOK]), (f"qs{s}", [P, 2, TOK]), (f"rv{s}", [P, TT + 1, UC])]
        (b0, kr0, qs0, rv0, b1, kr1, qs1, rv1, orec, D0, D1, D2, qt0, qt1, kt0, kt1, att, kh, eb, qh, khT, S, S0, S1, vblk) = stage(
            *g_names, ("orec", [P, KT, TOK]), ("D0", [P, TOK]), ("D1", [P, TOK]), ("D2", [P, TOK]), ("qt0", [P, HALF]), ("qt1", [P, HALF]),
            ("kt0", [P, TOK + SMP]), ("kt1", [P, TOK + SMP]), ("att", [P, TOK]), ("kh", [P, TOK]), ("eb", [P, TOK]),
            ("qh", [P, TOK]), ("khT", [P, TT + 1, P]), ("S", [P, TT, P]), ("S0", [P, NB, P]), ("S1", [P, NB, P]), ("vblk", [SMP, NB, P]))
        B, KR, QS, RV, D, QTL, KTL = [b0, b1], [kr0, kr1], [qs0, qs1], [rv0, rv1], [D0, D1, D2], [qt0, qt1], [kt0, kt1]
        osc = kh
        st = ExitStack()
        actR = sb("actR", [P, KT, 2, TOK], F32R, st)
        st.close()
        (_, *late) = stage(("gap3", [P, KT * 2 * TOK]), *[(f"late{i}", [P, UW]) for i in range(len(LATE))])
        (_, ysb) = stage(("gap2", [P, KT * 2 * TOK]), ("ysb", [P, TT + 1, DM]))

        PS = ctx.enter_context(nc.psum_tensor("PS", [P, 8, 512], F32))
        A = [PS[:, 4 + i, :] for i in range(4)]

        s_const = sem("s_const")
        s_x = sem("s_x")
        s_cache = sem("s_cache")
        s_raw = [sem(f"s_raw{i}") for i in range(2)]
        s_spill = sem("s_spill")
        s_back = sem("s_back")
        s_s0 = sem("s_s0")
        s_state_out = sem("s_state_out")
        s_win = sem("s_win")
        s_store = sem("s_store")
        s_mm = sem("s_mm")
        s_act_free = sem("s_act_free")
        s_dve_free = sem("s_dve_free")
        s_hi, s_lo = sem("s_hi"), sem("s_lo")
        s_pe_front, s_act_front, s_dve_front = sem("s_pe_front"), sem("s_act_front"), sem("s_dve_front")
        s_ada = [sem(f"s_ada{i}") for i in range(FRONT)]
        s_late = [sem(f"s_late{i}") for i in range(len(LATE))]
        s_sq, s_acc, s_stat, s_rb = sem("s_sq"), sem("s_acc"), sem("s_stat"), sem("s_rb")
        s_moved = sem("s_moved")
        s_xr, s_mod, s_hhi, s_hlo = sem("s_xr"), sem("s_mod"), sem("s_hhi"), sem("s_hlo")
        s_x2 = sem("s_x2")
        s_tanh, s_tused = sem("s_tanh"), sem("s_tused")
        s_sig, s_clamp, s_ln, s_scan = sem("s_sig"), sem("s_clamp"), sem("s_ln"), sem("s_scan")
        s_kq = sem("s_kq")
        s_qb = sem("s_qb")
        s_score, s_max, s_neg, s_exp = sem("s_score"), sem("s_max"), sem("s_neg"), sem("s_exp")
        s_pt, s_ptc, s_pv, s_o, s_ot, s_otc = (sem(n) for n in ("s_pt", "s_ptc", "s_pv", "s_o", "s_ot", "s_otc"))
        s_kw = sem("s_kw")
        s_D, s_E, s_Qt, s_Kt, s_lv, s_pred = (sem(n) for n in ("s_D", "s_E", "s_Qt", "s_Kt", "s_lv", "s_pred"))
        s_zero = sem("s_zero")
        s_dgm, s_dg = sem("s_dgm"), sem("s_dg")
        s_dx, s_ex, s_kh, s_qh = sem("s_dx"), sem("s_ex"), sem("s_kh"), sem("s_qh")
        s_kt, s_ktc, s_ds, s_st, s_vb = sem("s_kt"), sem("s_ktc"), sem("s_ds"), sem("s_st"), sem("s_vb")
        s_dss, s_sn = sem("s_dss"), sem("s_sn")
        s_out, s_osb, s_osq, s_ost, s_rbo, s_or = (sem(n) for n in ("s_out", "s_osb", "s_osq", "s_ost", "s_rbo", "s_or"))
        s_mix = sem("s_mix")
        s_sq2, s_ahi, s_alo = sem("s_sq2"), sem("s_ahi"), sem("s_alo")
        s_y, s_yt, s_yc = sem("s_y"), sem("s_yt"), sem("s_yc")
        s_dve, s_act, s_pool = sem("s_dve"), sem("s_act"), sem("s_pool")

        def ordered(eng, own):
            seen = {}

            def done(ins, s=None):
                s = own if s is None else s
                seen[s] = seen.get(s, 0) + 1
                ins.then_inc(s, 1)
                eng.wait_ge(s, seen[s])
            return done

        def pair_of(x):
            return PS[:, 2 * x.pair:2 * x.pair + 2, 0:HALF]

        def halves(ap):
            return ap.rearrange("p (a b) -> p a b", a=2)

        def split_index(n):
            return n % 2

        def weights(x, part, k, c0, cols=P):
            w = wR[split_index(x.split)]
            width = 512 if x.kind == "dn" else UC
            return w[:, part, k * width + c0:k * width + c0 + cols]

        def act_tile(x):
            n = 2 * x.i + x.n
            return (n // 4 % 2) * 4 + n % 4

        def count_kind(x, kinds):
            return sum(y.kind in kinds for y in TILES[:x.t + 1])

        def raw_loads(u):
            return sum(64 if UNITS[v][0] == "q" else 16 for v in RING if v <= u and SLOT[v] == SLOT[u])

        def prompt_step(s):
            hp, n = divmod(s - SAMP, TT)
            return hp, n, hp // 2, (0, 1) if n else (1,)

        kd = SEG["q"]
        block = ctx.enter_context(nc.Block())

        @block.sync
        def _(sp):
            sp.dma_start(cn[:], a["c"]).then_inc(s_const, 16)
            for name, at, n in (("norm_mix", "mix", 8), ("norm_mlp", "mlp", 8), ("hgrn_norm", "hgrn", 8),
                                ("hgrn_lb_logits", "lb", 8), ("b_ada", "bada", 48)):
                sp.dma_start(vrow[VN[at]:VN[at] + n, :], a[name][0].rearrange("(r p) -> r p", p=P)).then_inc(s_const, 16)
            sp.dma_start(vrow[VN["fin"]:VN["fin"] + 8, :], a["final_norm"].rearrange("(r p) -> r p", p=P)).then_inc(s_const, 16)
            sp.dma_start(ident[:], a["k_ident"]).then_inc(s_const, 16)

            def load(u):
                kind, i = UNITS[u]
                if u == FRONT + 1:
                    sp.wait_ge(s_dve_front, 6)
                if u in BEFORE:
                    if UNITS[BEFORE[u]][0] == "ada":
                        sp.wait_ge(s_mm, LAST[BEFORE[u]] + 1)
                    else:
                        sp.wait_ge(s_lo, 4 * (SPLITS.index(BEFORE[u]) + 1))
                s = s_raw[SLOT[u]]
                dst = raw[SLOT[u]][:].rearrange("p (k c) -> p k c", c=UC)
                if kind == "q":
                    d = raw[SLOT[u]][:].rearrange("p (k j g c) -> p k j g c", j=2, g=2, c=HD)
                    for j in range(2):
                        for g in range(2):
                            h = (2 * (i // 2) + g) * GRP + 2 * (i % 2) + j
                            sp.dma_start(d[:, :, j, g, :], w_in[:, h * HD:(h + 1) * HD].rearrange("(k p) c -> p k c", p=P)).then_inc(s, 16)
                    return
                if kind == "dn":
                    g, half = divmod(i, 2)
                    src = a["w_down"][0][g * 512:(g + 1) * 512, half * 512:(half + 1) * 512]
                    dst = raw[SLOT[u]][:].rearrange("p (k c) -> p k c", c=512)
                elif kind == "ada":
                    src = w_ada[:, i * UC:(i + 1) * UC]
                elif kind == "out":
                    src = a["w_out"][0][:, i * UC:(i + 1) * UC]
                elif kind == "up":
                    src = a["w_up"][0][:, i * UC:(i + 1) * UC]
                else:
                    at = SEG[kind] + i * UC
                    src = w_in[:, at:at + UC]
                sp.dma_start(dst, src.rearrange("(k p) c -> p k c", p=P)).then_inc(s, 16)

            def front_loads():
                sp.dma_start(resets_f[:], a["k_resets"]).then_inc(s_cache, 16)
                for i in range(TT):
                    sp.dma_start(xn[:, i, :], a["x_prompt"][0][i * P:(i + 1) * P, :]).then_inc(s_x, 16)
                sp.dma_start(xn[0:SMP, TT, :], a["x_sample"].rearrange("b t d -> (b t) d")).then_inc(s_x, 16)
                for i in range(FRONT):
                    sp.dma_start(ada[i][:].rearrange("p (k c) -> p k c", c=UC),
                                 w_ada[:, i * UC:(i + 1) * UC].rearrange("(k p) c -> p k c", p=P)).then_inc(s_ada[i], 16)
                load(FRONT)
                sp.dma_start(levels_f, a["k_levels"]).then_inc(s_cache, 16)
                sp.dma_start(own_seq[:], a["k_own_seq"]).then_inc(s_cache, 16)
                sp.dma_start(sink[:], a["attn_sinks"].to_broadcast([P, HEADS])).then_inc(s_cache, 16)
                sp.dma_start(sink_s[:], a["sink_rows"]).then_inc(s_cache, 16)

            def cache_loads():
                sp.wait_ge(s_mm, FRONT)
                sp.wait_ge(s_act_front, KT + 3)
                sp.dma_start(Kc[:], a["cache_win_k"][0].rearrange("b w h d -> w b (h d)")).then_inc(s_cache, 16)
                sp.dma_start(Vc[:], a["cache_win_v"][0].rearrange("b w h d -> w b (h d)")).then_inc(s_cache, 16)
                sp.dma_start(dist[:].rearrange("p a b -> p (a b)"), a["k_dist"]).then_inc(s_cache, 16)
                sp.dma_start(biasS[:], a["k_bias_s"]).then_inc(s_cache, 16)
            for ev, *x in walk():
                if ev == "load":
                    load(x[0])
                elif ev == "front":
                    front_loads()
                    load(FRONT + 1)
                    cache_loads()
                elif ev == "modulate" and x[0] == 0:
                    sp.wait_ge(s_xr, KT)
                    sp.dma_start(spill, xT[:].rearrange("p a b -> p (a b)")).then_inc(s_spill, 16)
                elif ev == "win":
                    for name in ("k", "v"):
                        sp.dma_start(o[f"win_{name}_sample"][0][:, 0:WIN - NT], a[f"cache_win_{name}"][0][:, NT:WIN]).then_inc(s_store, 16)
                    sp.wait_ge(s_kw, 2)
                    sp.dma_start(o["win_k_prompt"][0][0].rearrange("w h d -> w (h d)"), probs[0][:, 0:KV * HD]).then_inc(s_win, 16)
                    sp.dma_start(o["win_v_prompt"][0][0].rearrange("w h d -> w (h d)"), V[:, TT - 1, :]).then_inc(s_win, 16)
                    for b in range(NB):
                        rows = slice(b * NT, (b + 1) * NT)
                        sp.dma_start(o["win_k_sample"][0][b, WIN - NT:WIN].rearrange("w h d -> w (h d)"), probs[1][rows, 0:KV * HD]).then_inc(s_win, 16)
                        sp.dma_start(o["win_v_sample"][0][b, WIN - NT:WIN].rearrange("w h d -> w (h d)"), V[rows, TT, :]).then_inc(s_win, 16)
                elif ev == "g_start":
                    r = x[0]
                    if r == 0:
                        sp.wait_ge(s_win, (2 + 2 * NB) * 16)
                        sp.wait_ge(s_otc, STEPS - PREP)
                    else:
                        sp.wait_ge(s_out, r)
                        sp.wait_ge(s_sn, 2 * r)
                    sp.dma_start(S0[:], a["state_hgrn"][0][:, r].rearrange("b k v -> k b v")).then_inc(s_s0, 16)
                elif ev == "g_norm":
                    r = x[0]
                    sp.wait_ge(s_sn, 2 * (r + 1))
                    sp.wait_ge(s_st, r + 1)
                    sp.dma_start(o["hgrn_sample"][0][:, r].rearrange("b k v -> k b v"), S1[:]).then_inc(s_state_out, 16)
                    sp.dma_start(o["hgrn_prompt"][0][0, r], S[:, TT - 1, :]).then_inc(s_state_out, 16)
                elif ev == "evac" and x[0].kind == "rg" and x[0].t == LAST[x[0].u] and x[0].i == 3:
                    sp.wait_ge(s_mix, 2 * RH)
                    sp.wait_ge(s_spill, 16)
                    sp.dma_start(xT[:].rearrange("p a b -> p (a b)"), spill).then_inc(s_back, 16)
                    sp.wait_ge(s_or, RH)
                    sp.wait_ge(s_state_out, 32 * RH)
                    for i, u in enumerate(LATE):
                        at = UNITS[u][1] * UC
                        sp.dma_start(late[i][:].rearrange("p (k c) -> p k c", c=UC),
                                     w_ada[:, at:at + UC].rearrange("(k p) c -> p k c", p=P)).then_inc(s_late[i], 16)
                elif ev == "final":
                    for n, k in enumerate((KT // 2, KT)):
                        sp.wait_ge(s_yc, 2 * k)
                        lo, hi = n * DM // 2, (n + 1) * DM // 2
                        sp.dma_start(o["y_prompt"][0].rearrange("(i p) d -> p i d", p=P)[:, :, lo:hi], ysb[:, 0:TT, lo:hi]).then_inc(s_store, 16)
                        sp.dma_start(o["y_sample"].rearrange("b t d -> (b t) d")[:, lo:hi], ysb[0:SMP, TT, lo:hi]).then_inc(s_store, 16)
            sp.wait_ge(s_store, 6 * 16)
            sp.wait_ge(s_state_out, 32 * RH)
            sp.wait_ge(s_win, (2 + 2 * NB) * 16)

        @block.tensor
        def _(pe):
            state = {"stat": 0}

            def front():
                pe.wait_ge(s_const, 8 * 16)
                pe.transpose(PS[:, 0, 0:NVEC], vrow[:, :], ident[0:NVEC, 0:NVEC]).then_inc(s_pe_front, 1)
                pe.wait_ge(s_dve_front, 1)
                for k in range(KT):
                    mm = pe.transpose(PS[:, 1, k * NSEQ:(k + 1) * NSEQ], cn[:, k * P:(k + 1) * P], ident[0:NSEQ, 0:NSEQ])
                mm.then_inc(s_pe_front, 1)
                pe.wait_ge(s_x, (TT + 1) * 16)
                pe.wait_ge(s_dve_front, 3)
                for k in range(KT):
                    bank = (2 + k) % 8
                    for i in range(TT):
                        mm = pe.transpose(PS[:, bank, i * P:(i + 1) * P], xn[:, i, k * P:(k + 1) * P], ident[:])
                    mm.then_inc(s_pe_front, 1)
                pe.wait_ge(s_act_front, 3)
                for k in range(KT):
                    mm = pe.transpose(PS[:, 2, k * SMP:(k + 1) * SMP], xn[0:SMP, TT, k * P:(k + 1) * P], ident[0:SMP, 0:SMP])
                mm.then_inc(s_pe_front, 1)
                pe.wait_ge(s_act_front, KT + 3)

            def stats(n):
                pe.wait_ge(s_acc, (n + 1) * (KT - 1))
                for h in range(2):
                    mm = pe.matmul(A[h][:, 0:HALF], ones[:], rb[:, h * HALF:(h + 1) * HALF], start=True, stop=True)
                mm.then_inc(s_stat, 1)

            def tile_part(x, c):
                b0_, b1_ = 2 * x.pair, 2 * x.pair + 1
                if c == 0:
                    if x.t >= 2:
                        y = TILES[x.t - 2]
                        reader = READER[y.kind]
                        pe.wait_ge(dict(act=s_act_free, dve=s_dve_free, tanh=s_tused)[reader], count_read(y.t, reader))
                    if x.kind == "ada" and x.u < FRONT:
                        pe.wait_ge(s_ada[x.u], 16)
                    elif x.u in LATE:
                        pe.wait_ge(s_late[LATE.index(x.u)], 16)
                    elif x.kind == "ada":
                        pe.wait_ge(s_raw[SLOT[x.u]], raw_loads(x.u))
                    elif x.n == 0:
                        pe.wait_ge(s_lo, 4 * (x.split + 1))
                    if x.kind == "out" and x.i == 0 and x.n == 0:
                        pe.wait_ge(s_mix, 2 * RH)
                if x.kind == "ada":
                    w = ada[x.u] if x.u < FRONT else late[LATE.index(x.u)] if x.u in LATE else raw[SLOT[x.u]]
                    for m in range(2):
                        for k in range(KT):
                            mm = pe.matmul(PS[:, b0_, m * NSEQ:(m + 1) * NSEQ], w[:, k * UC + m * P:k * UC + (m + 1) * P],
                                           cT[:, k, :], start=(k == 0), stop=(k == KT - 1))
                    mm.then_inc(s_mm, 1)
                    return
                if x.kind in ("v", "ri"):
                    for k in range(4 * c, 4 * c + 4):
                        lhs = [hR[:, part, k * TOK + x.n * P:k * TOK + (x.n + 1) * P] for part in range(2)]
                        for n, (l, w) in enumerate(((0, 0), (0, 1), (1, 0))):
                            mm = pe.matmul(PS[:, b0_, 0:UC], lhs[l], weights(x, w, k, 0, UC),
                                           start=(k == 0 and n == 0), stop=(k == KT - 1 and n == 2))
                    if c == 1:
                        mm.then_inc(s_mm, 1)
                    return
                if (x.kind, x.i) in JOINT:
                    if x.n:
                        return
                    if c == 0:
                        y = TILES[x.t - 1]
                        pe.wait_ge(dict(act=s_act_free, dve=s_dve_free, tanh=s_tused)[READER[y.kind]], count_read(y.t, READER[y.kind]))
                    for k in (2 * c, 2 * c + 1):
                        pe.wait_ge(s_hlo, (KT if x.kind == "up" else 0) + k + 1)
                        for m in range(2):
                            for h in range(2):
                                for n, (w, r) in enumerate(((0, 0), (0, 1), (1, 0))):
                                    rhs = hR[:, r, k * TOK + h * HALF:k * TOK + (h + 1) * HALF]
                                    mm = pe.matmul(PS[:, 2 * ((x.pair + m) % 2) + h, 0:HALF], weights(x, w, k, m * P), rhs,
                                                   start=(k == 0 and n == 0), stop=(k == KT - 1 and n == 2))
                    if c == 3:
                        mm.then_inc(s_mm, 2)
                    return
                if x.kind == "dn":
                    h, ks, col = c, range(4), x.n * P
                else:
                    h, ks, col = c // 2, range(4 * (c % 2), 4 * (c % 2) + 4), x.n * P
                last = KT - 1 if x.kind != "dn" else 3
                for k in ks:
                    if x.kind == "dn":
                        slot_ = (x.i // 2 % 2) * 4 + k
                        if x.n == 0 and h == 0 and x.i % 2 == 0:
                            pe.wait_ge(s_alo, 4 * (x.i // 2) + k + 1)
                        rhs = [actR[:, slot_, part, h * HALF:(h + 1) * HALF] for part in range(2)]
                    elif x.kind == "out":
                        rhs = [actR[:, k, part, h * HALF:(h + 1) * HALF] for part in range(2)]
                    else:
                        rhs = [hR[:, part, k * TOK + h * HALF:k * TOK + (h + 1) * HALF] for part in range(2)]
                    for n, (w, r) in enumerate(((0, 0), (0, 1), (1, 0))):
                        mm = pe.matmul(PS[:, 2 * x.pair + h, 0:HALF], weights(x, w, k, col), rhs[r],
                                       start=(k == 0 and n == 0), stop=(k == last and n == 2))
                if c == CHUNKS.get(x.kind, 4) - 1:
                    mm.then_inc(s_mm, 1)

            def a_score(s):
                if s >= 1:
                    pe.wait_ge(s_max, s)
                if s < PREP:
                    if s == 0:
                        pe.wait_ge(s_cache, 9 * 16)
                    for i in range(2):
                        for T in range(2):
                            mm = pe.transpose(A[0][:, (2 * i + T) * P:(2 * i + T + 1) * P], Kc[:, 2 * s + i, T * P:(T + 1) * P], ident[:])
                    mm.then_inc(s_score, 1)
                    return
                if s < SAMP:
                    b = s - PREP
                    if b == 0:
                        pe.wait_ge(s_qb, 1)
                    for T in range(2):
                        pe.matmul(A[0][:, 0:P], Qblk[:, T, b, :], KcT[:, b, T, :], start=(T == 0), stop=(T == 1))
                    for T in range(2):
                        mm = pe.matmul(A[0][:, P:P + SMP], Qblk[:, T, b, :], kT[:, T, SEQ:TOK], start=(T == 0), stop=(T == 1))
                    mm.then_inc(s_score, 1)
                    return
                hp, n, g, kts = prompt_step(s)
                rows = slice((g % 2) * HD, (g % 2 + 1) * HD)
                for e in range(2):
                    j = 2 * (hp % 2) + e
                    q = qT[rows, (g // 2) * GRP + j, n * P:(n + 1) * P]
                    k0 = (n - 1 + kts[0]) * P
                    mm = pe.matmul(A[0][:, e * 2 * P + kts[0] * P:(e + 1) * 2 * P], q, kT[rows, g // 2, k0:(n + 1) * P], start=True, stop=True)
                mm.then_inc(s_score, 1)

            def a_probs(s):
                pe.wait_ge(s_exp, s - PREP + 1)
                if s > PREP:
                    pe.wait_ge(s_ptc, s - PREP)
                p = probs[s % 2]
                if s < SAMP:
                    pe.transpose(A[1][:, 0:P], p[:, 0:P], ident[:])
                    mm = pe.transpose(A[1][0:SMP, P:2 * P], p[:, P:P + SMP], ident[:])
                else:
                    for kt in prompt_step(s)[3]:
                        for e in range(2):
                            mm = pe.transpose(A[1][:, (2 * kt + e) * P:(2 * kt + e + 1) * P], p[:, (2 * e + kt) * P:(2 * e + kt + 1) * P], ident[:])
                mm.then_inc(s_pt, 1)

            def a_value(s):
                pe.wait_ge(s_ptc, s - PREP + 1)
                if s > PREP:
                    pe.wait_ge(s_o, s - PREP)
                if s < SAMP:
                    b = s - PREP
                    pe.matmul(A[2][:, 0:KV * HD], probsT[:, 0:P], Vc[:, b, :], start=True, stop=False)
                    mm = pe.matmul(A[2][:, 0:KV * HD], probsT[0:SMP, P:2 * P], V[0:SMP, TT, :], start=False, stop=True)
                else:
                    hp, n, g, kts = prompt_step(s)
                    for e in range(2):
                        for kt in kts:
                            mm = pe.matmul(A[2][:, e * HD:(e + 1) * HD], probsT[:, (2 * kt + e) * P:(2 * kt + e + 1) * P],
                                           V[:, n - 1 + kt, g * HD:(g + 1) * HD], start=(kt == kts[0]), stop=(kt == 1))
                mm.then_inc(s_pv, 1)

            def a_turn(s):
                pe.wait_ge(s_o, s - PREP + 1)
                if s > PREP:
                    pe.wait_ge(s_otc, s - PREP)
                if s < SAMP:
                    mm = pe.transpose(A[3][0:HD, 0:P], osb[:, 0:HD], ident[:])
                else:
                    mm = pe.transpose(A[3][:, 0:P], osb[:, 0:P], ident[:])
                mm.then_inc(s_ot, 1)

            def win():
                pe.wait_ge(s_max, STEPS)
                for T in range(2):
                    pe.transpose(A[0][:, T * P:(T + 1) * P], kT[:, T, SEQ - P:SEQ], ident[:])
                for T in range(2):
                    mm = pe.transpose(A[0][0:SMP, (2 + T) * P:(3 + T) * P], kT[:, T, SEQ:TOK], ident[:])
                mm.then_inc(s_score, 1)

            def g_diag(r):
                k, q = KR[r // 2 % 2], QS[r // 2 % 2]
                pe.wait_ge(s_tused, TANH.index(LAST[UNITS.index(("rq", r // 2))]) + 1)
                pe.wait_ge(s_otc, STEPS - PREP)
                if r:
                    pe.wait_ge(s_sn, 2 * r)
                for c in range(TT):
                    cols = slice(c * P, (c + 1) * P)
                    pe.matmul(A[2][:, cols], k[:, r % 2, cols], q[:, r % 2, cols], start=True, stop=True)
                pe.matmul(A[3][0:SMP, 0:SMP], k[:, r % 2, SEQ:TOK], q[:, r % 2, SEQ:TOK], start=True, stop=True).then_inc(s_dgm, 1)

            def g_level(r, l):
                n = r * NL + l
                pe.wait_ge(s_Qt, n + 1)
                pe.wait_ge(s_Kt, n + 1)
                if n >= 2:
                    pe.wait_ge(s_pred, n - 1)
                if l < 2 and r:
                    pe.wait_ge(s_rbo, r)
                elif l < 2:
                    pe.wait_ge(s_kw, 2)
                bank, q, k = A[l % 2], QTL[n % 2], KTL[n % 2]
                for c in range(TT):
                    mm = pe.matmul(bank[:, c * HD:(c + 1) * HD], k[:, c * P:(c + 1) * P], q[:, c * HD:(c + 1) * HD], start=True, stop=True)
                if LEVELS[l] < NT:
                    mm = pe.matmul(bank[:, SEQ // 2:HALF], k[:, SEQ:TOK + SMP], q[:, SEQ // 2:HALF], start=True, stop=True)
                mm.then_inc(s_lv, 1)

            def g_keys(r):
                pe.wait_ge(s_kh, r + 1)
                pe.wait_ge(s_dg, r + 1)
                for c in range(TT):
                    pe.transpose(A[2][:, c * P:(c + 1) * P], kh[:, c * P:(c + 1) * P], ident[:])
                pe.transpose(A[3][0:SMP, 0:P], kh[:, SEQ:TOK], ident[:]).then_inc(s_kt, 1)

            def g_state(r):
                pe.wait_ge(s_ktc, 2 * r + 2)
                v = RV[r // 2 % 2]
                e = (r % 2) * P
                for c in range(TT):
                    mm = pe.matmul(A[2][:, c * P:(c + 1) * P], khT[:, c, :], v[:, c, e:e + P], start=True, stop=True)
                mm.then_inc(s_ds, 1)

            def g_sample(r, h):
                pe.wait_ge(s_vb, r + 1)
                pe.wait_ge(s_ktc, 2 * r + 2)
                if h:
                    pe.wait_ge(s_st, r + 1)
                pe.matmul(A[3 - h][:, :], khT[0:SMP, TT, :], vblk[:, 4 * h:4 * h + 4, :].rearrange("p b v -> p (b v)"),
                          start=True, stop=True).then_inc(s_dss, 1)

            def g_out(r):
                v, e = RV[r // 2 % 2], (r % 2) * P
                pe.wait_ge(s_pred, (r + 1) * NL)
                pe.wait_ge(s_qh, r + 1)
                pe.wait_ge(s_st, r + 1)
                pe.wait_ge(s_s0, 16 * (r + 1))
                for c in range(TT):
                    cols = slice(c * P, (c + 1) * P)
                    if c:
                        pe.matmul(A[0][:, cols], S[:, c - 1, :], qh[:, cols], start=True, stop=False)
                    pe.matmul(A[0][:, cols], v[:, c, e:e + P], att[:, cols], start=(c == 0), stop=True)
                pe.matmul(A[1][:, 0:SMP], v[0:SMP, TT, e:e + P], att[0:SMP, SEQ:TOK], start=True, stop=False, skip_group_check=True)
                for b in range(NB):
                    mm = pe.matmul(A[1][:, b * NT:(b + 1) * NT], S0[:, b, :], qh[:, SEQ + b * NT:SEQ + (b + 1) * NT],
                                   start=False, stop=(b == NB - 1), skip_group_check=True)
                mm.then_inc(s_out, 1)

            def g_norm(r):
                pe.wait_ge(s_osq, r + 1)
                for h in range(2):
                    mm = pe.matmul(A[h][:, 0:HALF], ones[:], att[:, h * HALF:(h + 1) * HALF], start=True, stop=True)
                mm.then_inc(s_ost, 1)

            def final():
                for k in range(KT):
                    pe.wait_ge(s_y, k + 1)
                    if k >= 2:
                        pe.wait_ge(s_yc, 2 * (k - 1))
                    bank = k % 2
                    for i in range(TT):
                        mm = pe.transpose(PS[:, bank, i * P:(i + 1) * P], tmp[k % 2][:, i * P:(i + 1) * P], ident[:])
                    mm = pe.transpose(PS[0:SMP, 2 + bank, 0:P], tmp[k % 2][:, SEQ:TOK], ident[:])
                    mm.then_inc(s_yt, 1)

            for ev, *x in walk():
                if ev == "front":
                    front()
                elif ev == "norm":
                    stats(0)
                elif ev == "finish_stats":
                    stats(*x)
                elif ev == "mm":
                    tile_part(*x)
                elif ev == "a_score":
                    a_score(*x)
                elif ev == "a_probs":
                    a_probs(*x)
                elif ev == "a_value":
                    a_value(*x)
                elif ev == "a_turn":
                    a_turn(*x)
                elif ev == "win":
                    win()
                elif ev == "g_diag":
                    g_diag(*x)
                elif ev == "g_level":
                    g_level(*x)
                elif ev == "g_keys":
                    g_keys(*x)
                elif ev == "g_state":
                    g_state(*x)
                elif ev == "g_sample":
                    g_sample(*x)
                elif ev == "g_out":
                    g_out(*x)
                elif ev == "g_norm":
                    g_norm(*x)
                elif ev == "final":
                    pe.wait_ge(s_dve_free, count_read(len(TILES) - 1, "dve"))
                    final()

        @block.scalar
        def _(act):
            done = ordered(act, s_act)
            seen = {"tanh": 0}

            def front():
                act.wait_ge(s_const, 8 * 16)
                done(act.activation(cgate[:], cn[:], ACT.Tanh, scale=0.5), s_act_front)
                act.wait_ge(s_dve_front, 4)
                done(act.activation(lb[:], lb[:], ACT.Exp), s_act_front)
                for k in range(KT):
                    act.wait_ge(s_pe_front, 3 + k)
                    done(act.activation(xT[:, k, 0:SEQ], PS[:, (2 + k) % 8, :], ACT.Copy), s_act_front)
                act.wait_ge(s_pe_front, 3 + KT)
                done(act.activation(xT[:, :, SEQ:TOK], PS[:, 2, :].rearrange("p (k t) -> p k t", t=SMP), ACT.Copy), s_act_front)

            def squares(n, k):
                if k >= 3:
                    act.wait_ge(s_acc, n * (KT - 1) + k - 2)
                if n:
                    act.wait_ge(s_x2, (n - 1) * KT + k + 1)
                if n and k == KT - 1:
                    done(act.activation(warm[:], eps[:, 0:1], ACT.Ln))
                done(act.activation((tmp[2 + k % 2] if k else rb)[:], xT[:, k, :], ACT.Square), s_sq)

            def rms(n):
                act.wait_ge(s_stat, n + 1)
                act.wait_ge(s_dve_front, 4)
                for h in range(2):
                    done(act.activation(rb[:, h * HALF:(h + 1) * HALF], A[h][:, 0:HALF], ACT.Ln, scale=1.0 / DM, bias=eps[:, 0:1]))
                done(act.activation(rb[:], rb[:], ACT.Exp, scale=-0.5), s_rb)

            def modulate(n):
                sh, sc = (0, KT) if n == 0 else (3 * KT, 4 * KT)
                for k in range(KT):
                    act.wait_ge(s_xr, n * KT + k + 1)
                    h = tmp[k % 4]
                    done(act.activation(h[:, 0:SEQ], h[:, 0:SEQ], ACT.Identity, scale=mods[:, sc + k, 0:1], bias=mods[:, sh + k, 0:1]), s_mod)

            def evac(x):
                src = pair_of(x)
                if READER[x.kind] == "dve":
                    return
                act.wait_ge(s_mm, x.t + 1)
                if x.kind in ("k", "q"):
                    dst = kT[:, x.n, :] if x.kind == "k" else qT[:, 2 * x.i + x.n, :]
                    done(act.activation(halves(dst), src, ACT.Copy), s_act_free)
                elif x.kind in ("v", "ri"):
                    rows = P if x.n < TT else SMP
                    dst = V if x.kind == "v" else RV[x.i % 2]
                    done(act.activation(dst[0:rows, x.n, :], PS[0:rows, 2 * x.pair, 0:UC], ACT.Copy), s_act_free)
                elif x.kind == "rf":
                    n = 2 * x.i + x.n
                    if n == 0:
                        act.wait_ge(s_hlo, KT)
                    if n >= 2:
                        act.wait_ge(s_scan, n - 1)
                    done(act.activation(halves(tmp[x.n][:]), src, ACT.Sigmoid), s_act_free)
                    if x.n == 1:
                        for e in range(2):
                            r = 2 * x.i + e
                            act.wait_ge(s_clamp, r + 1)
                            done(act.activation(tmp[e][:], tmp[e][:], ACT.Ln, scale=omlb[:, r:r + 1], bias=lb[:, r:r + 1]), s_ln)
                elif x.kind in ("rq", "ga", "gr", "rg"):
                    n = seen["tanh"]
                    seen["tanh"] += 1
                    if n >= 2:
                        act.wait_ge(s_tused, n - 1)
                    s = s_act_free if x.kind in ("ga", "gr") else s_tanh
                    done(act.activation(halves(tmp[2 + n % 2][:]), src, ACT.Tanh, scale=0.5), s)
                elif x.kind == "up":
                    n = 2 * x.i + x.n
                    if n >= 2:
                        act.wait_ge(s_alo, n - 1)
                    t = tmp[n % 2][:]
                    done(act.activation(halves(t), src, ACT.Relu), s_act_free)
                    done(act.activation(t, t, ACT.Square), s_sq2)

            def a_exp(s):
                q = s - PREP
                act.wait_ge(s_neg, q + 1)
                m, p = small[:, s % 4], probs[s % 2]
                if s < SAMP:
                    done(act.activation(p[:, 0:P + SMP], p[:, 0:P + SMP], ACT.Exp, bias=m[:, 1, 0:1], accum_out=m[:, 3, 0:1]))
                    done(act.activation(m[:, 2, 0:1], m[:, 2, 0:1], ACT.Exp), s_exp)
                    return
                k0 = prompt_step(s)[3][0] * P
                for e in range(2):
                    t = p[:, e * 2 * P + k0:(e + 1) * 2 * P]
                    done(act.activation(t, t, ACT.Exp, bias=m[:, 1, e:e + 1], accum_out=m[:, 3, e:e + 1]))
                done(act.activation(m[:, 2, :], m[:, 2, :], ACT.Exp), s_exp)

            def a_take(s):
                act.wait_ge(s_pt, s - PREP + 1)
                if s > PREP:
                    act.wait_ge(s_pv, s - PREP)
                if s < SAMP:
                    done(act.activation(probsT[:, 0:P], A[1][:, 0:P], ACT.Copy))
                    done(act.activation(probsT[0:SMP, P:2 * P], A[1][0:SMP, P:2 * P], ACT.Copy), s_ptc)
                    return
                k0 = prompt_step(s)[3][0] * 2 * P
                done(act.activation(probsT[:, k0:4 * P], A[1][:, k0:4 * P], ACT.Copy), s_ptc)

            def a_put(s):
                act.wait_ge(s_ot, s - PREP + 1)
                if s == PREP:
                    act.wait_ge(s_spill, 16)
                if s < SAMP:
                    b = s - PREP
                    src = A[3][0:HD, 0:P].rearrange("p (k e t) -> p k e t", e=2, t=NT)
                    cols = slice(SEQ + b * NT, SEQ + (b + 1) * NT)
                    done(act.activation(attnT[0:HD, :, cols], src[:, :, 0, :], ACT.Copy))
                    done(act.activation(attnT[HD:P, :, cols], src[:, :, 1, :], ACT.Copy), s_otc)
                    return
                hp, n, g, kts = prompt_step(s)
                done(act.activation(attnT[:, hp, n * P:(n + 1) * P], A[3][:, 0:P], ACT.Copy), s_otc)

            def g_exp(r, l):
                m, i = LEVELS[l], r * NL + l
                n = TOK if m < NT else SEQ
                act.wait_ge(s_D, i + 1)
                d = D[i % 3][:, 0:n].rearrange("p (a m) -> p a m", m=2 * m)
                done(act.activation(d[:, :, m:2 * m], d[:, :, m:2 * m], ACT.Exp))
                done(act.activation(d[:, :, 0:m], d[:, :, 0:m], ACT.Exp, scale=-1.0), s_E)

            def g_hats(r):
                done(act.activation(eb[:], B[r // 2 % 2][:, r % 2, :], ACT.Exp))
                act.wait_ge(s_dx, r + 1)
                done(act.activation(kh[:], kh[:], ACT.Exp), s_ex)

            def g_keys(r):
                act.wait_ge(s_kt, r + 1)
                done(act.activation(khT[:, 0:TT, :], A[2].rearrange("p (c k) -> p c k", k=P), ACT.Copy), s_ktc)
                done(act.activation(khT[0:SMP, TT, :], A[3][0:SMP, 0:P], ACT.Copy), s_ktc)

            def g_out(r):
                act.wait_ge(s_out, r + 1)
                done(act.activation(osc[:, 0:SEQ], A[0][:, :], ACT.Copy, scale=QSCALE))
                done(act.activation(osc[:, SEQ:TOK], A[1][:, 0:SMP], ACT.Copy, scale=QSCALE), s_osb)
                done(act.activation(att[:], osc[:], ACT.Square), s_osq)

            def g_norm(r):
                act.wait_ge(s_ost, r + 1)
                if r:
                    act.wait_ge(s_or, r)
                for h in range(2):
                    done(act.activation(rb[:, h * HALF:(h + 1) * HALF], A[h][:, 0:HALF], ACT.Ln, scale=1.0 / P, bias=eps[:, 0:1]))
                done(act.activation(rb[:], rb[:], ACT.Exp, scale=-0.5), s_rbo)

            def final():
                for k in range(KT):
                    act.wait_ge(s_yt, k + 1)
                    bank = k % 2
                    done(act.activation(ysb[:, 0:TT, k * P:(k + 1) * P], PS[:, bank, :].rearrange("p (i c) -> p i c", c=P), ACT.Copy), s_yc)
                    done(act.activation(ysb[0:SMP, TT, k * P:(k + 1) * P], PS[0:SMP, 2 + bank, 0:P], ACT.Copy), s_yc)

            for ev, *x in walk():
                if ev == "front":
                    front()
                elif ev == "norm":
                    for k in range(KT):
                        squares(0, k)
                    rms(0)
                elif ev == "stats":
                    squares(*x)
                elif ev == "finish_stats":
                    rms(*x)
                elif ev == "modulate":
                    modulate(*x)
                elif ev == "evac":
                    evac(*x)
                elif ev == "a_exp":
                    a_exp(*x)
                elif ev == "a_take":
                    a_take(*x)
                elif ev == "a_put":
                    a_put(*x)
                elif ev == "g_exp":
                    g_exp(*x)
                elif ev == "g_hats":
                    g_hats(*x)
                elif ev == "g_keys":
                    g_keys(*x)
                elif ev == "g_out":
                    g_out(*x)
                elif ev == "g_norm":
                    g_norm(*x)
                elif ev == "final":
                    final()

        @block.vector
        def _(dve):
            done = ordered(dve, s_dve)
            seen = {"tanh": 0}

            def per_seq(ap):
                return ap.rearrange("p (b t) -> p b t", t=NT)

            def mod_s(k):
                return mods[:, k, 1:NSEQ].unsqueeze(2).to_broadcast([P, NB, NT])

            def front():
                done(dve.memset(ones[:], 1.0))
                done(dve.memset(eps[:], EPS))
                done(dve.memset(hR[:, :, KT * TOK:].bitcast(F32), 0.0))
                dve.wait_ge(s_act_front, 1)
                done(dve.scalar_tensor_tensor(cn[:], cgate[:], 1.0, cn[:], ALU.add, ALU.mult))
                done(dve.tensor_scalar(cn[:], cn[:], 0.5, None, ALU.mult), s_dve_front)
                dve.wait_ge(s_pe_front, 1)
                done(dve.tensor_copy(vec[:], PS[:, 0, 0:NVEC]), s_dve_front)
                dve.wait_ge(s_pe_front, 2)
                done(dve.tensor_copy(cT[:].rearrange("p k c -> p (k c)"), PS[:, 1, 0:KT * NSEQ]), s_dve_front)
                lo = vec[:, VN["lb"]:VN["lb"] + KT]
                done(dve.tensor_tensor(lb[:], lo, lo, ALU.subtract), s_dve_front)
                dve.wait_ge(s_act_front, 2)
                done(dve.reciprocal(omlb[:], lb[:]))
                done(dve.tensor_tensor(omlb[:], lb[:], omlb[:], ALU.mult))
                done(dve.tensor_tensor(lb[:], omlb[:], omlb[:], ALU.subtract))
                done(dve.tensor_scalar(omlb[:], lb[:], -1.0, 1.0, ALU.mult, ALU.add))
                done(dve.tensor_scalar(nomlb[:], omlb[:], -1.0, None, ALU.mult))
                dve.wait_ge(s_cache, 5 * 16)
                done(dve.tensor_copy(levels[:].rearrange("p a b -> p (a b)"), levels_f[:]), s_dve_front)
                done(dve.tensor_copy(resets[:], resets_f[:]), s_dve_front)

            def modulate(n):
                sh, sc, g = (0, KT, VN["mix"]) if n == 0 else (3 * KT, 4 * KT, VN["mlp"])
                done(dve.scalar_tensor_tensor(mods[:, sc:sc + KT, :], mods[:, sc:sc + KT, :], 1.0,
                                              vec[:, g:g + KT].unsqueeze(2).to_broadcast([P, KT, NSEQ]), ALU.add, ALU.mult))
                dve.wait_ge(s_rb, n + 1)
                if n:
                    dve.wait_ge(s_mm, max(x.t for x in TILES if x.kind == "rg") + 1)

                def normalise(k):
                    if k >= 4:
                        dve.wait_ge(s_hlo, n * KT + k - 3)
                    done(dve.tensor_tensor(tmp[k % 4][:], xT[:, k, :], rb[:], ALU.mult), s_xr)

                for k in range(3):
                    normalise(k)
                for k in range(KT):
                    if k + 3 < KT:
                        normalise(k + 3)
                    h = tmp[k % 4]
                    hs = per_seq(h[:, SEQ:TOK])
                    done(dve.tensor_tensor(hs, hs, mod_s(sc + k), ALU.mult))
                    done(dve.tensor_tensor(hs, hs, mod_s(sh + k), ALU.add))
                    dve.wait_ge(s_mod, n * KT + k + 1)
                    done(dve.tensor_copy(hR[:, 0, k * TOK:(k + 1) * TOK], h[:]), s_hhi)

            def hi(n):
                u = SPLITS[n]
                dve.wait_ge(s_raw[SLOT[u]], raw_loads(u))
                if n >= 2:
                    dve.wait_ge(s_mm, LAST[SPLITS[n - 2]] + 1)
                done(dve.tensor_copy(wR[split_index(n)][:, 0, :], raw[SLOT[u]][:]), s_hi)

            def residual(x, m, gate):
                b0_ = 2 * x.pair
                dve.wait_ge(s_mm, x.t + 1)
                cut = SEQ - HALF
                done(dve.scalar_tensor_tensor(xT[:, m, 0:HALF], PS[:, b0_, 0:HALF], mods[:, gate + m, 0:1], xT[:, m, 0:HALF], ALU.mult, ALU.add))
                done(dve.scalar_tensor_tensor(xT[:, m, HALF:SEQ], PS[:, b0_ + 1, 0:cut], mods[:, gate + m, 0:1], xT[:, m, HALF:SEQ], ALU.mult, ALU.add))
                done(dve.tensor_tensor(per_seq(tmp_s[:]), per_seq(PS[:, b0_ + 1, cut:HALF]), mod_s(gate + m), ALU.mult), s_dve_free)
                last = xT[:, m, SEQ:TOK]
                signal = x.kind == "out" or x.i >= 14
                done(dve.tensor_tensor(last, last, tmp_s[:], ALU.add), s_x2 if signal else None)

            def evac(x):
                if x.kind == "ada":
                    m = 2 * x.i
                    dve.wait_ge(s_mm, x.t + 1)
                    done(dve.tensor_tensor(mods[:, m:m + 2, :], PS[:, 2 * x.pair, 0:2 * NSEQ].rearrange("p (m c) -> p m c", c=NSEQ),
                                           vec[:, VN["bada"] + m:VN["bada"] + m + 2].unsqueeze(2).to_broadcast([P, 2, NSEQ]), ALU.add), s_dve_free)
                elif x.kind == "rf":
                    n, e = 2 * x.i + x.n, x.n
                    t = tmp[e]
                    dve.wait_ge(s_act_free, count_read(x.t, "act"))
                    done(dve.tensor_scalar(KR[x.i % 2][:, e, :], t[:], 1.0, nomlb[:, n:n + 1], ALU.subtract, ALU.mult))
                    done(dve.tensor_scalar(t[:], t[:], LEAST, None, ALU.max), s_clamp)
                    if e == 1:
                        if n == 1:
                            dve.wait_ge(s_cache, 9 * 16)
                        for f in range(2):
                            dve.wait_ge(s_ln, 2 * x.i + f + 1)
                            done(dve.tensor_tensor_scan(B[x.i % 2][:, f, :], resets[:], tmp[f][:], 0.0, ALU.mult, ALU.add), s_scan)
                elif x.kind in ("rq", "ga", "gr", "rg"):
                    n = seen["tanh"]
                    seen["tanh"] += 1
                    t = tmp[2 + n % 2]
                    if x.kind in ("ga", "gr"):
                        dve.wait_ge(s_act_free, count_read(x.t, "act"))
                    else:
                        dve.wait_ge(s_tanh, sum(TILES[y].kind in ("rq", "rg") for y in TANH[:n + 1]))
                    r = 2 * x.i + x.n
                    if x.kind == "rq":
                        done(dve.scalar_tensor_tensor(halves(QS[x.i % 2][:, x.n, :]), halves(t[:]), 1.0, pair_of(x), ALU.add, ALU.mult), s_tused)
                    elif x.kind == "ga":
                        done(dve.scalar_tensor_tensor(attnT[:, r, :], t[:], 1.0, attnT[:, r, :], ALU.add, ALU.mult), s_tused)
                    elif x.kind == "gr":
                        done(dve.scalar_tensor_tensor(orec[:, r, :], t[:], 1.0, orec[:, r, :], ALU.add, ALU.mult), s_tused)
                    else:
                        m = tmp[x.n]
                        done(dve.scalar_tensor_tensor(halves(m[:]), halves(t[:]), 1.0, pair_of(x), ALU.add, ALU.mult), s_tused)
                        done(dve.tensor_tensor(m[:], m[:], orec[:, r, :], ALU.mult))
                        done(dve.scalar_tensor_tensor(m[:], m[:], 0.5, attnT[:, r, :], ALU.mult, ALU.add))
                        done(dve.tensor_scalar(actR[:, r, 0, :], m[:], 0.5, None, ALU.mult), s_mix)
                        done(dve.scalar_tensor_tensor(actR[:, r, 1, :], m[:], 0.5, actR[:, r, 0, :].bitcast(F32), ALU.mult, ALU.subtract), s_mix)
                elif x.kind == "up":
                    n = 2 * x.i + x.n
                    if n == 0:
                        dve.wait_ge(s_mm, max(y.t for y in TILES if y.kind == "out") + 1)
                    if n >= 8:
                        dve.wait_ge(s_mm, LAST[UNITS.index(("dn", 2 * (n // 4 - 2) + 1))] + 1)
                    dve.wait_ge(s_sq2, n + 1)
                    done(dve.tensor_copy(actR[:, act_tile(x), 0, :], tmp[n % 2][:]), s_ahi)
                elif x.kind == "out":
                    if x.i == 0 and x.n == 0:
                        dve.wait_ge(s_back, 16)
                    residual(x, 2 * x.i + x.n, 2 * KT)
                elif x.kind == "dn":
                    residual(x, 4 * (x.i % 2) + x.n, 5 * KT)

            def q_blocks():
                dve.wait_ge(s_act_front, KT + 3)
                done(dve.memset(Qblk[:].rearrange("p a b c -> p (a b c)"), 0.0))
                dve.wait_ge(s_act_free, count_read(LAST[UNITS.index(("q", 3))], "act"))
                for g in range(KV):
                    rows, T = slice((g % 2) * HD, (g % 2 + 1) * HD), g // 2
                    for j in range(GRP):
                        c = g * GRP * NT + j * NT
                        src = per_seq(qT[rows, T * GRP + j, SEQ:TOK])
                        ins = dve.tensor_copy(Qblk[rows, T, :, c:c + NT], src)
                        done(ins, s_qb if (g, j) == (KV - 1, GRP - 1) else None)

            def a_max(s):
                dve.wait_ge(s_score, s + 1)
                if s < PREP:
                    done(dve.tensor_copy(KcT[:, 2 * s:2 * s + 2, :, :].rearrange("p b t w -> p (b t w)"), A[0]), s_max)
                    return
                if s - PREP >= 2:
                    dve.wait_ge(s_pt, s - PREP - 1)
                m, p = small[:, s % 4], probs[s % 2]
                if s < SAMP:
                    b = s - PREP
                    done(dve.tensor_tensor_reduce(p[:, 0:P], A[0][:, 0:P], biasS[:, 0:P], HD ** -0.5, sink_s[:, 0:1], ALU.add, ALU.max, m[:, 5, 0:1]))
                    new = biasS[:, P + 56 - b * NT:P + 56 - b * NT + SMP]
                    done(dve.tensor_tensor_reduce(p[:, P:P + SMP], A[0][:, P:P + SMP], new, HD ** -0.5, m[:, 5, 0:1], ALU.add, ALU.max, m[:, 0, 0:1]), s_max)
                    done(dve.tensor_tensor(m[:, 2, 0:1], sink_s[:, 0:1], m[:, 0, 0:1], ALU.subtract))
                    done(dve.tensor_scalar(m[:, 1, 0:1], m[:, 0, 0:1], -1.0, None, ALU.mult), s_neg)
                    return
                hp, n, g, kts = prompt_step(s)
                k0 = kts[0] * P
                if n == 0:
                    for e in range(2):
                        slope = 2.0 ** (-8.0 * (2 * hp + e + 1) / HEADS)
                        done(dve.scalar_tensor_tensor(biasP[:, e, :], dist[:, 0, :], -slope * HD ** 0.5, dist[:, 1, :], ALU.mult, ALU.add))
                for e in range(2):
                    cols = slice(e * 2 * P + k0, (e + 1) * 2 * P)
                    h = 2 * hp + e
                    done(dve.tensor_tensor_reduce(p[:, cols], A[0][:, cols], biasP[:, e, k0:2 * P], HD ** -0.5, sink[:, h:h + 1],
                                                  ALU.add, ALU.max, m[:, 0, e:e + 1]), s_max if e else None)
                done(dve.tensor_tensor(m[:, 2, :], sink[:, 2 * hp:2 * hp + 2], m[:, 0, :], ALU.subtract))
                done(dve.tensor_scalar(m[:, 1, :], m[:, 0, :], -1.0, None, ALU.mult), s_neg)

            def a_scale(s):
                m = small[:, s % 4]
                w = 1 if s < SAMP else 2
                dve.wait_ge(s_exp, s - PREP + 1)
                done(dve.tensor_tensor(m[:, 4, 0:w], m[:, 3, 0:w], m[:, 2, 0:w], ALU.add))
                done(dve.reciprocal(m[:, 4, 0:w], m[:, 4, 0:w]))
                dve.wait_ge(s_pv, s - PREP + 1)
                if s > PREP:
                    dve.wait_ge(s_ot, s - PREP)
                if s < SAMP:
                    for g in range(KV):
                        rows = slice(g * GRP * NT, (g + 1) * GRP * NT)
                        done(dve.tensor_scalar(osb[rows, 0:HD], A[2][rows, g * HD:(g + 1) * HD], m[rows, 4, 0:1], None, ALU.mult),
                             s_o if g == KV - 1 else None)
                    return
                done(dve.tensor_tensor(osb[:].rearrange("p (e d) -> p e d", e=2), A[2][:, 0:P].rearrange("p (e d) -> p e d", e=2),
                                       m[:, 4, :].unsqueeze(2).to_broadcast([P, 2, HD]), ALU.mult), s_o)

            def win():
                dve.wait_ge(s_score, STEPS + 1)
                dve.wait_ge(s_pt, STEPS - PREP)
                done(dve.tensor_copy(probs[0][:, 0:KV * HD], A[0][:, 0:KV * HD]), s_kw)
                done(dve.tensor_copy(probs[1][0:SMP, 0:KV * HD], A[0][0:SMP, KV * HD:2 * KV * HD]), s_kw)

            def g_operands(r, l):
                m, n = LEVELS[l], r * NL + l
                w = TOK if m < NT else SEQ
                view = lambda t: t[:, 0:w].rearrange("p (a m) -> p a m", m=2 * m)
                q, k = QS[r // 2 % 2][:, r % 2, :], KR[r // 2 % 2][:, r % 2, :]
                d = view(D[n % 3])
                if n < 2:
                    if n == 0:
                        dve.wait_ge(s_win, (2 + 2 * NB) * 16)
                        dve.wait_ge(s_otc, STEPS - PREP)
                    done(dve.memset(KTL[n % 2][:], 0.0))
                dve.wait_ge(s_E, n + 1)
                if n >= 2:
                    dve.wait_ge(s_lv, n - 1)
                done(dve.tensor_tensor(QTL[n % 2][:, 0:w // 2].rearrange("p (a m) -> p a m", m=m), view(q)[:, :, m:2 * m], d[:, :, m:2 * m], ALU.mult), s_Qt)
                done(dve.tensor_tensor(view(KTL[n % 2])[:, :, 0:m], view(k)[:, :, 0:m], d[:, :, 0:m], ALU.mult), s_Kt)

            def g_diag(r):
                dve.wait_ge(s_dgm, r + 1)
                if r:
                    dve.wait_ge(s_ost, r)
                done(dve.tensor_tensor(att[:, 0:SEQ].rearrange("p (c t) -> p c t", t=P), A[2].rearrange("p (c t) -> p c t", t=P),
                                       ident[:].unsqueeze(1).to_broadcast([P, TT, P]), ALU.mult))
                if r == 0:
                    done(dve.memset(att[SMP:P, SEQ:TOK], 0.0))
                done(dve.tensor_tensor(att[0:SMP, SEQ:TOK], A[3][0:SMP, 0:SMP], ident[0:SMP, 0:SMP], ALU.mult), s_dg)

            def g_level(r, l):
                m, n = LEVELS[l], r * NL + l
                w = TOK if m < NT else SEQ
                dve.wait_ge(s_lv, n + 1)
                half = lambda t: t[:, 0:w // 2].rearrange("p (a m) -> p a m", m=m)
                done(dve.copy_predicated(att[:, 0:w].rearrange("p (a m) -> p a m", m=2 * m)[:, :, m:2 * m], half(levels[:, l, :]), half(A[l % 2])), s_pred)

            def g_hats(r):
                dve.wait_ge(s_ex, r + 1)
                s = r // 2 % 2
                if r:
                    dve.wait_ge(s_out, r)
                done(dve.tensor_tensor(qh[:], QS[s][:, r % 2, :], eb[:], ALU.mult), s_qh)
                done(dve.tensor_tensor(kh[:], KR[s][:, r % 2, :], kh[:], ALU.mult), s_kh)

            def g_keys(r):
                e = (r % 2) * P
                if r:
                    dve.wait_ge(s_dss, 2 * r)
                done(dve.tensor_tensor(vblk[:], RV[r // 2 % 2][0:SMP, TT, e:e + P].unsqueeze(1).to_broadcast([SMP, NB, P]),
                                       own_seq[:].unsqueeze(2).to_broadcast([SMP, NB, P]), ALU.mult), s_vb)

            def g_state(r):
                dve.wait_ge(s_ds, r + 1)
                if r:
                    dve.wait_ge(s_state_out, 32 * r)
                done(dve.tensor_copy(S[:, 0, :], A[2][:, 0:P]))
                for c in range(1, TT):
                    last = eb[:, (c + 1) * P - 1:(c + 1) * P]
                    done(dve.scalar_tensor_tensor(S[:, c, :], S[:, c - 1, :], last, A[2][:, c * P:(c + 1) * P], ALU.mult, ALU.add),
                         s_st if c == TT - 1 else None)

            def g_sample(r, h):
                dve.wait_ge(s_dss, 2 * r + h + 1)
                for b in range(4 * h, 4 * h + 4):
                    last = eb[:, SEQ + (b + 1) * NT - 1:SEQ + (b + 1) * NT]
                    if b == 0:
                        dve.wait_ge(s_s0, 16 * (r + 1))
                    done(dve.scalar_tensor_tensor(S1[:, b, :], S0[:, b, :], last, A[3 - h][:, (b % 4) * P:(b % 4 + 1) * P], ALU.mult, ALU.add),
                         s_sn if b % 4 == 3 else None)

            def g_norm(r):
                dve.wait_ge(s_rbo, r + 1)
                done(dve.scalar_tensor_tensor(orec[:, r, :], osc[:], vec[:, VN["hgrn"] + r:VN["hgrn"] + r + 1], rb[:], ALU.mult, ALU.mult), s_or)

            def final():
                dve.wait_ge(s_rb, 3)
                for k in range(KT):
                    if k >= 2:
                        dve.wait_ge(s_yt, k - 1)
                    done(dve.scalar_tensor_tensor(tmp[k % 2][:], xT[:, k, :], vec[:, VN["fin"] + k:VN["fin"] + k + 1], rb[:], ALU.mult, ALU.mult), s_y)

            for ev, *x in walk():
                if ev == "front":
                    front()
                elif ev == "modulate":
                    modulate(*x)
                elif ev == "hi":
                    hi(*x)
                elif ev == "evac":
                    evac(*x)
                elif ev == "q_blocks":
                    q_blocks()
                elif ev == "a_max":
                    a_max(*x)
                elif ev == "a_scale":
                    a_scale(*x)
                elif ev == "win":
                    win()
                elif ev == "g_operands":
                    g_operands(*x)
                elif ev == "g_diag":
                    g_diag(*x)
                elif ev == "g_level":
                    g_level(*x)
                elif ev == "g_hats":
                    g_hats(*x)
                elif ev == "g_keys":
                    g_keys(*x)
                elif ev == "g_state":
                    g_state(*x)
                elif ev == "g_sample":
                    g_sample(*x)
                elif ev == "g_norm":
                    g_norm(*x)
                elif ev == "final":
                    final()

        @block.gpsimd
        def _(pool):
            done = ordered(pool, s_pool)

            def lo(n, q):
                pool.wait_ge(s_hi, n + 1)
                w = wR[split_index(n)]
                cols = slice(q * UW // 4, (q + 1) * UW // 4)
                done(pool.tensor_tensor(w[:, 1, cols], raw[SLOT[SPLITS[n]]][:, cols], w[:, 0, cols].bitcast(F32), ALU.subtract), s_lo)

            def squares(n, k):
                if k:
                    pool.wait_ge(s_sq, n * KT + k + 1)
                    done(pool.tensor_tensor(rb[:], rb[:], tmp[2 + k % 2][:], ALU.add), s_acc)

            def modulate(n):
                for k in range(KT):
                    pool.wait_ge(s_hhi, n * KT + k + 1)
                    cols = slice(k * TOK, (k + 1) * TOK)
                    done(pool.tensor_tensor(hR[:, 1, cols], tmp[k % 4][:], hR[:, 0, cols].bitcast(F32), ALU.subtract), s_hlo)

            def g_diff(r, l):
                m, n = LEVELS[l], r * NL + l
                if n == 0:
                    pool.wait_ge(s_win, (2 + 2 * NB) * 16)
                    pool.wait_ge(s_otc, STEPS - PREP)
                if l == 0:
                    pool.wait_ge(s_scan, r + 1)
                if n >= 3:
                    pool.wait_ge(s_Kt, n - 2)
                w = TOK if m < NT else SEQ
                bv = B[r // 2 % 2][:, r % 2, 0:w].rearrange("p (a m) -> p a m", m=2 * m)
                done(pool.tensor_tensor(D[n % 3][:, 0:w].rearrange("p (a m) -> p a m", m=2 * m), bv,
                                        bv[:, :, m - 1:m].to_broadcast([P, w // (2 * m), 2 * m]), ALU.subtract), s_D)

            def g_hats(r):
                if r:
                    pool.wait_ge(s_or, r)
                for lo, hi, m, last in ((0, SEQ, P, False), (SEQ, TOK, NT, True)):
                    bv = B[r // 2 % 2][:, r % 2, lo:hi].rearrange("p (a m) -> p a m", m=m)
                    done(pool.tensor_tensor(kh[:, lo:hi].rearrange("p (a m) -> p a m", m=m), bv[:, :, m - 1:m].to_broadcast([P, (hi - lo) // m, m]),
                                            bv, ALU.subtract), s_dx if last else None)

            def evac(x):
                if x.kind == "up":
                    n = 2 * x.i + x.n
                    pool.wait_ge(s_ahi, n + 1)
                    a_ = actR[:, act_tile(x)]
                    done(pool.tensor_tensor(a_[:, 1, :], tmp[n % 2][:], a_[:, 0, :].bitcast(F32), ALU.subtract), s_alo)

            for ev, *x in walk():
                if ev == "lo":
                    lo(*x)
                elif ev == "norm":
                    for k in range(KT):
                        squares(0, k)
                elif ev == "stats":
                    squares(*x)
                elif ev == "modulate":
                    modulate(*x)
                elif ev == "g_diff":
                    g_diff(*x)
                elif ev == "g_hats":
                    g_hats(*x)
                elif ev == "evac":
                    evac(*x)


def constants():
    import numpy as np
    far = -1e30 * HD ** 0.5
    q, kk = np.arange(P)[:, None], np.arange(2 * P)[None]
    d = q + P - kk
    dist = np.stack([d, np.where((d >= 0) & (d <= WIN), 0.0, far)], 1).astype(np.float32)
    slope = (2.0 ** (-8.0 * np.arange(1, HEADS + 1) / HEADS))[np.arange(P) // NT][:, None]
    t = (np.arange(P) % NT)[:, None]
    dc = WIN + t - np.arange(P)[None]
    old = np.where((dc >= 0) & (dc <= WIN), -slope * dc * HD ** 0.5, far)
    i = np.arange(120)[None] - 56
    dn = t - i
    new = np.where((i >= 0) & (i < NT) & (dn >= 0), -slope * dn * HD ** 0.5, far)
    lv = np.zeros((P, NL, HALF), np.float32)
    s = np.arange(P)
    for l, m in enumerate(LEVELS):
        tt = np.arange(TOK).reshape(-1, 2 * m)[:, m:].ravel() if TOK % (2 * m) == 0 else np.arange(SEQ).reshape(-1, 2 * m)[:, m:].ravel()
        if m >= NT:
            tt = tt[tt < SEQ]
        for c, t_ in enumerate(tt):
            w = t_ % P
            lv[:, l, c] = (s // (2 * m) == w // (2 * m)) & (s % (2 * m) < m)
            if t_ >= SEQ:
                lv[SMP:, l, c] = 0
    resets = np.ones((P, TOK), np.float32)
    resets[:, 0:SEQ:P] = 0
    resets[:, SEQ::NT] = 0
    own = (np.arange(SMP)[:, None] // NT == np.arange(NB)[None]).astype(np.float32)
    return dict(k_ident=np.eye(P, dtype=np.float32), k_dist=dist.reshape(P, -1), k_bias_s=np.concatenate([old, new], 1).astype(np.float32),
                k_levels=lv.reshape(P, -1), k_resets=resets, k_own_seq=own)


_INS = ["x_prompt", "x_sample", "cache_win_k", "cache_win_v", "state_hgrn", "norm_mix", "norm_mlp", "w_ada", "b_ada",
        "w_in", "attn_sinks", "hgrn_lb_logits", "hgrn_norm", "w_out", "w_up", "w_down", "final_norm"]
_OUTS = dict(y_prompt=(1, SEQ, DM), y_sample=(NB, NT, DM), win_k_prompt=(1, 1, WIN, KV, HD), win_v_prompt=(1, 1, WIN, KV, HD),
             hgrn_prompt=(1, 1, RH, P, P), win_k_sample=(1, NB, WIN, KV, HD), win_v_sample=(1, NB, WIN, KV, HD),
             hgrn_sample=(1, NB, RH, P, P))


def kernel(**inputs):
    import numpy as np
    import concourse.bacc as bacc
    from concourse.bass_utils import run_bass_kernel_spmd

    nc = bacc.Bacc("TRN2", target_bir_lowering=False, num_devices=1, dynamic_dma_scratch_size=8192)
    given = {n: np.ascontiguousarray(inputs[n]) for n in _INS}
    given["c"] = np.concatenate([np.asarray(inputs["c_prompt"]), np.asarray(inputs["c_sample"])], 0)
    given["sink_rows"] = np.repeat(np.asarray(inputs["attn_sinks"])[0], NT)[:, None]
    given.update(constants())
    arrays, ins = {}, {}
    for name, v in given.items():
        arrays[f"in_{name}"] = v
        ins[name] = nc.dram_tensor(f"in_{name}", v.shape, mybir.dt.from_np(v.dtype), kind="ExternalInput").ap()
    outs = {n: nc.dram_tensor(f"out_{n}", s, F32, kind="ExternalOutput").ap() for n, s in _OUTS.items()}
    program(nc, ins, outs)
    r = run_bass_kernel_spmd(nc, [arrays], core_ids=[0])
    return tuple(r.results[0][f"out_{n}"] for n in _OUTS)
```

```python
import concourse.bass as bass
from concourse import mybir
from contextlib import ExitStack

F32 = mybir.dt.float32
F32R = mybir.dt.float32r
U8 = mybir.dt.uint8
ALU = mybir.AluOpType
ACT = mybir.ActivationFunctionType
AX = mybir.AxisListType

P = 128
DM = 1024
KT = DM // P
SEQ = 512
NB, NT = 8, 8
SMP = NB * NT
TOK = SEQ + SMP
HALF = TOK // 2
TT = SEQ // P
HEADS, KV, HD = 16, 4, 64
GRP = HEADS // KV
WIN = 128
RH = 8
DFF = 4 * DM
EPS = 1e-6
UC = 256
UW = KT * UC
NSEQ = 1 + NB
SEG = dict(q=0, k=1024, v=1280, rq=1536, rf=2560, ri=3584, rg=4608, ga=5632, gr=6656)
LEVELS = (64, 32, 16, 8, 4, 2, 1)
NL = len(LEVELS)
QSCALE = 0.5 * P ** -0.5
LEAST = 1e-19
VN = dict(mix=0, mlp=8, hgrn=16, fin=24, lb=32, bada=40)
NVEC = 88


def units():
    w_in = [("k", 0), ("v", 0)] + [("q", i) for i in range(4)]
    for p in (0, 1):
        w_in += [("rf", p), ("rq", p), ("ri", p)]
    w_in += [("ga", i) for i in range(4)]
    for p in (2, 3):
        w_in += [("rf", p), ("rq", p), ("ri", p)]
    for p in range(4):
        w_in += [("gr", p), ("rg", p)]
    out = [("ada", i) for p in range(4) for i in (p, p + 4)]
    rest = [("ada", i) for i in range(8, 20)]
    for u in w_in:
        out.append(u)
        if rest:
            out.append(rest.pop(0))
    out += [("out", i) for i in range(4)]
    out += [("ada", i) for i in range(20, 24)]
    out += [("up", 0), ("up", 1)]
    for g in range(1, 8):
        out += [("up", 2 * g), ("up", 2 * g + 1), ("dn", 2 * g - 2), ("dn", 2 * g - 1)]
    return out + [("dn", 14), ("dn", 15)]


UNITS = units()
NTILES = dict(ada=1, v=5, ri=5, dn=4)
READER = dict(ada="dve", k="act", v="act", q="act", rf="act", ri="act", ga="act", gr="act", up="act",
              rq="tanh", rg="tanh", out="dve", dn="dve")
CHUNKS = dict(ada=1, v=2, ri=2, dn=2)


SUMMED = 4
CG = 32
FRONT = 8
ADA = [u for u, x in enumerate(UNITS) if x[0] == "ada"]
LATE = [u for u, x in enumerate(UNITS) if x[0] == "ada" and x[1] >= 20]
MID = [u for u in ADA if u >= FRONT and u not in LATE]
RING = [u for u in range(FRONT, len(UNITS)) if u not in ADA]
SLOT = {u: n % 2 for n, u in enumerate(RING)}
BEFORE = {u: RING[n - 2] for n, u in enumerate(RING) if n >= 2}
AFTER = {u: RING[n + 2] for n, u in enumerate(RING) if n + 2 < len(RING)}
JOINT = (("k", 0), ("up", 0))


class Tile:

    def __init__(self, t, u, kind, i, n, split):
        self.t, self.u, self.kind, self.i, self.n, self.split = t, u, kind, i, n, split
        self.pair = t % 2 + (2 if u < FRONT else 0)


def tiles():
    out, split = [], 0
    for u, (kind, i) in enumerate(UNITS):
        for n in range(NTILES.get(kind, 2)):
            out.append(Tile(len(out), u, kind, i, n, split))
        split += kind != "ada"
    return out


TILES = tiles()
SPLITS = [u for u, (kind, _) in enumerate(UNITS) if kind != "ada"]
LAST = {u: max(x.t for x in TILES if x.u == u) for u in range(len(UNITS))}
TANH = [x.t for x in TILES if x.kind in ("rq", "ga", "gr", "rg")]


def count_read(t, reader):
    if reader == "tanh":
        return TANH.index(t) + 1
    return sum(READER[x.kind] == reader for x in TILES[:t + 1])


PREP, SAMP = 4, 4 + NB
STEPS = SAMP + (HEADS // 2) * TT


def prep_slots():
    for s in range(PREP):
        yield [("a_score", s), ("a_max", s)]


def attention_slots():
    for s in range(PREP, STEPS + 3):
        ev = []
        if s >= PREP + 3:
            ev += [("a_turn", s - 3), ("a_put", s - 3)]
        if PREP + 2 <= s < STEPS + 2:
            ev += [("a_value", s - 2), ("a_scale", s - 2)]
        if PREP + 1 <= s < STEPS + 1:
            ev += [("a_probs", s - 1), ("a_take", s - 1)]
        if s < STEPS:
            ev = [("a_score", s), ("a_max", s)] + ev + [("a_exp", s)]
        yield ev
    yield [("win", 0)]


def hgrn_slots(pair):
    first, second = 2 * pair, 2 * pair + 1

    def at(n):
        return divmod(n, NL)[0] + first, n % NL

    yield [("g_start", first), ("g_diff", first, 0), ("g_diff", first, 1), ("g_exp", first, 0), ("g_diff", first, 2),
           ("g_operands", first, 0), ("g_exp", first, 1)]
    yield []
    yield []
    for r in (first, second):
        if r == second:
            yield []
        for k in range(NL + 2):
            ev = []
            if k == 0:
                ev += [("g_diag", r)]
            if k < NL:
                n = (r - first) * NL + k
                if n + 1 < 2 * NL:
                    ev += [("g_operands", *at(n + 1))]
                if k == 2:
                    ev += [("g_products", r)]
                ev += [("g_level", r, k)]
                if n + 2 < 2 * NL:
                    ev += [("g_exp", *at(n + 2))]
                if n + 3 < 2 * NL:
                    ev += [("g_diff", *at(n + 3))]
            if k == 0 and r == second:
                ev += [("g_scale", first)]
            if k == 1:
                ev += [("g_hats", r)]
            if k == 3:
                ev += [("g_keys", r)]
            if k == 4:
                ev += [("g_state", r)]
            if k in (5, 6):
                ev += [("g_sample", r, k - 5)]
            if k == NL:
                ev += [("g_out", r)]
                if r == first:
                    ev += [("g_start", second)]
            if k == NL + 1:
                ev += [("g_norm", r)]
                if r == second:
                    ev += [("g_scale", r)]
            yield ev


def walk():
    first = {}
    for x in TILES:
        first.setdefault((x.kind, x.i), x.t)
    work = [[prep_slots(), first["q", 0], first["rq", 0]],
            [attention_slots(), first["rq", 0], first["ga", 1]],
            [hgrn_slots(0), first["ga", 0], first["rf", 2]],
            [hgrn_slots(1), first["ga", 0], first["rf", 3]],
            [hgrn_slots(2), first["rf", 3], first["gr", 0]],
            [hgrn_slots(3), first["gr", 0], first["gr", 2]]]

    def slot(t):
        while work and work[0][1] <= t:
            ev = next(work[0][0], None)
            if ev is not None:
                return ev
            work.pop(0)
        return []

    yield ("front",)
    k_tile = TILES[first["k", 0]]
    pairs = FRONT // 2
    for p in range(pairs):
        for x in TILES[2 * p:2 * p + 2]:
            yield ("mm", x, 0)
            yield ("ada_part", x)
        if p == 0:
            yield ("hi", 0)
            yield ("lo", 0, 0)
        for x in TILES[2 * p:2 * p + 2]:
            yield ("ada_sum", x)
            yield ("evac", x)
        if p == 0:
            yield ("norm",)
            yield ("load", AFTER[SPLITS[0]])
            yield ("load_mid", MID[0])
            yield ("caches",)
        if p >= 1:
            yield ("modulate", 0, 2 * (p - 1))
        if p >= 2:
            yield ("mm", k_tile, p - 2)
    yield ("modulate", 0, 2 * (pairs - 1))
    yield ("mm", k_tile, pairs - 2)
    pending = None
    merging = None
    scanning = None
    turning = None
    for x in TILES[FRONT:]:
        while work and work[0][2] <= x.t:
            for ev in work.pop(0)[0]:
                yield from ev
        joint = (x.kind, x.i) in JOINT
        if pending and joint:
            yield ("ada_sum", pending)
            yield ("evac", pending)
            pending = None
        if x.kind == "ada" and x.i == 20:
            n = SPLITS.index(UNITS.index(("up", 1)))
            yield ("hi", n)
            for q in range(4):
                yield ("lo", n, q)
            yield ("load", AFTER[SPLITS[n]])
        if x.kind == "ada" and x.i == 21:
            yield ("finish_stats", 1)
        if x.kind == "up" and x.i == 0 and x.n == 0:
            for k in range(0, KT, 2):
                yield ("modulate", 1, k)
        if x.kind == "q" and x.n == 0 and x.i == 1:
            yield ("tables",)
        for c in range(CHUNKS.get(x.kind, 4)):
            if x is not k_tile or c == 3:
                yield ("mm", x, c)
            if pending and c == (0 if x.kind == "ada" else 2 if x.kind != "v" and x.kind != "ri" else 1):
                yield ("ada_sum", pending)
                yield ("evac", pending)
                pending = None
            if merging and c in (0, 2):
                yield ("merge", merging, c // 2)
                merging = None if c else merging
            if scanning is not None and x.kind != "ada":
                yield ("scan", scanning)
                scanning = None
            at = x.n * CHUNKS.get(x.kind, 4) + c
            if at < 4 and (x.kind, x.i) != ("up", 0) and x.kind != "ada" and x.split + 1 < len(SPLITS):
                if at == 0:
                    yield ("hi", x.split + 1)
                yield ("lo", x.split + 1, at)
                if at == 3 and SPLITS[x.split + 1] in AFTER:
                    yield ("load", AFTER[SPLITS[x.split + 1]])
            yield from slot(x.t)
        if turning is not None:
            yield ("y_turn", turning)
        if x.kind == "ada":
            yield ("ada_part", x)
            pending = x
        else:
            yield ("evac", x)
        if turning is not None:
            yield ("y_put", turning)
        if x.kind == "rf" and x.n == 1:
            scanning = x.i
        if x.kind == "rg":
            merging = x
            if x.t == LAST[x.u] and x.i == 3:
                yield ("merge", x, 0)
                yield ("merge", x, 1)
                merging = None
        if x.u in MID[:-1]:
            yield ("load_mid", MID[MID.index(x.u) + 1])
        if x.kind == "q" and x.n == 1:
            yield ("q_blocks", x.i)
        if x.kind == "q" and x.n == 1 and x.i == 2:
            yield ("masks",)
        if x.kind == "out":
            yield ("stats", 1, 2 * x.i + x.n)
        if x.kind == "dn" and x.i >= 14:
            turning = 4 * (x.i - 14) + x.n
            yield ("stats", 2, turning)
    yield ("finish_stats", 2)
    yield ("y_turn", KT - 1)
    yield ("y_put", KT - 1)
    yield ("final",)


def program(nc, a, o):
    w_in, w_ada = a["w_in"][0], a["w_ada"][0]
    spill = nc.dram_tensor("residual", [P, KT * TOK], F32).ap()

    ctx = ExitStack()
    with ctx:
        def sb(name, shape, dt=F32, stack=ctx):
            return stack.enter_context(nc.sbuf_tensor(name, shape, dt))

        def sem(name):
            return ctx.enter_context(nc.semaphore(name))

        ident = sb("ident", [P, P])
        ones = sb("ones", [P, P])
        levels = sb("levels", [P, NL, HALF], U8)
        resets = sb("resets", [P, TOK], U8)
        own_seq = sb("own_seq", [SMP, NB])
        vec = sb("vec", [P, NVEC])
        mods = sb("mods", [P, 6 * KT, NSEQ])
        cT = sb("cT", [P, KT, CG])
        collect = sb("collect", [P, NSEQ])
        part = [sb(f"part{i}", [P, UC]) for i in range(2)]
        sink = sb("sink", [P, HEADS])
        sink_s = sb("sink_s", [P, 1])
        eps = sb("eps", [P, 1])
        lb = sb("lb", [P, KT])
        omlb = sb("omlb", [P, KT])
        nomlb = sb("nomlb", [P, KT])
        small = sb("small", [P, 4, 6, 2])
        tmp_s = sb("tmp_s", [P, SMP])
        rbt = sb("rbt", [P, TT + 1])
        rb = sb("rb", [P, TOK])
        tmp = [sb(f"tmp{i}", [P, TOK]) for i in range(4)]
        hR = sb("hR", [P, 2, KT * TOK + SMP], F32R)
        raw = [sb(f"raw{i}", [P, UW]) for i in range(2)]
        wR = [sb(f"wR{i}", [P, 2, UW], F32R) for i in range(2)]
        xT = sb("xT", [P, KT, TOK])
        attnT = xT

        def stage(*tensors):
            st, out = ExitStack(), []
            for name, shape in tensors:
                out.append(sb(name, shape, F32, st))
            st.close()
            return out

        ZS = [2 * TOK, 2 * TOK, 2 * TOK, 5 * UC]
        (xn, cn, cgate, vrow, *ada) = stage(
            ("xn", [P, TT + 1, DM]), ("cn", [NSEQ, DM]), ("cgate", [NSEQ, DM]), ("vrow", [NVEC, P]),
            *[(f"ada{i}", [P, UW]) for i in range(FRONT)])
        (xhat0,) = stage(("xhat0", [P, KT, TOK]))
        (Kc, levels_f, resets_f, _, KcT, Qblk, _, Vc, biasP, dist, pr0, pr1, probsT, qT, kT, V, biasS, osb, mid) = stage(
            ("Kc", [P, NB, KV * HD]), ("levels_f", [P, NL * HALF]), ("resets_f", [P, TOK]),
            ("gap0", [P, sum(ZS) - NB * KV * HD - NL * HALF - TOK]),
            ("KcT", [P, NB, 2, P]), ("Qblk", [P, 2, NB, P]), ("gap1", [P, sum(ZS) - 4 * NB * P]),
            ("Vc", [P, NB, KV * HD]), ("biasP", [P, 2, 2 * P]), ("dist", [P, 2, 2 * P]),
            ("pr0", [P, 512]), ("pr1", [P, 512]), ("probsT", [P, 512]),
            ("qT", [P, KT, TOK]), ("kT", [P, 2, TOK]), ("V", [P, TT + 1, KV * HD]), ("biasS", [P, P + 120]),
            ("osb", [P, P]), ("mid", [P, UW]))
        probs = [pr0, pr1]
        g_names = []
        for s in range(2):
            g_names += [(f"b{s}", [P, 2, TOK]), (f"kr{s}", [P, 2, TOK]), (f"qs{s}", [P, 2, TOK]), (f"rv{s}", [P, TT + 1, UC])]
        (b0, kr0, qs0, rv0, b1, kr1, qs1, rv1, orec, D0, D1, D2, qt0, qt1, kt0, kt1, att, kh, eb, qh, khT, S, S0, S1, vblk) = stage(
            *g_names, ("orec", [P, KT, TOK]), ("D0", [P, TOK]), ("D1", [P, TOK]), ("D2", [P, TOK]), ("qt0", [P, HALF]), ("qt1", [P, HALF]),
            ("kt0", [P, TOK + SMP]), ("kt1", [P, TOK + SMP]), ("att", [P, TOK]), ("kh", [P, TOK]), ("eb", [P, TOK]),
            ("qh", [P, TOK]), ("khT", [P, TT + 1, P]), ("S", [P, TT, P]), ("S0", [P, NB, P]), ("S1", [P, NB, P]), ("vblk", [SMP, NB, P]))
        B, KR, QS, RV, D, QTL, KTL = [b0, b1], [kr0, kr1], [qs0, qs1], [rv0, rv1], [D0, D1, D2], [qt0, qt1], [kt0, kt1]
        osc = kh
        st = ExitStack()
        actR = sb("actR", [P, KT, 2, TOK], F32R, st)
        st.close()
        (_, *late, xhat1) = stage(("gap3", [P, KT * 2 * TOK]), *[(f"late{i}", [P, UW]) for i in range(len(LATE))], ("xhat1", [P, KT, TOK]))
        xhat = [xhat0, xhat1]
        (_, ysb) = stage(("gap2", [P, KT * 2 * TOK]), ("ysb", [P, TT + 1, DM]))
        xw = xhat1

        PS = ctx.enter_context(nc.psum_tensor("PS", [P, 8, 512], F32))
        A = [PS[:, 4 + i, :] for i in range(4)]

        s_const = sem("s_const")
        s_x = sem("s_x")
        s_cache, s_tables = sem("s_cache"), sem("s_tables")
        s_raw = [sem(f"s_raw{i}") for i in range(2)]
        s_spill = sem("s_spill")
        s_back = sem("s_back")
        s_s0 = sem("s_s0")
        s_state_out = sem("s_state_out")
        s_win = sem("s_win")
        s_store = sem("s_store")
        s_mm = sem("s_mm")
        s_act_free = sem("s_act_free")
        s_dve_free = sem("s_dve_free")
        s_hi, s_lo = sem("s_hi"), sem("s_lo")
        s_pe_front, s_act_front, s_dve_front = sem("s_pe_front"), sem("s_act_front"), sem("s_dve_front")
        s_ada = [sem(f"s_ada{i}") for i in range(FRONT)]
        s_mid = sem("s_mid")
        s_late = [sem(f"s_late{i}") for i in range(len(LATE))]
        s_sq, s_acc, s_stat, s_rb = sem("s_sq"), sem("s_acc"), sem("s_stat"), sem("s_rb")
        s_part, s_asum = sem("s_part"), sem("s_asum")
        s_xe = sem("s_xe")
        s_hs = sem("s_hs")
        s_xr, s_hhi, s_hlo = sem("s_xr"), sem("s_hhi"), sem("s_hlo")
        s_vec = sem("s_vec")
        s_x2 = sem("s_x2")
        s_tanh, s_tused = sem("s_tanh"), sem("s_tused")
        s_clamp, s_ln, s_scan = sem("s_clamp"), sem("s_ln"), sem("s_scan")
        s_qb = sem("s_qb")
        s_score, s_max, s_neg, s_exp = sem("s_score"), sem("s_max"), sem("s_neg"), sem("s_exp")
        s_pt, s_ptc, s_pv, s_o, s_ot, s_otc = (sem(n) for n in ("s_pt", "s_ptc", "s_pv", "s_o", "s_ot", "s_otc"))
        s_kw = sem("s_kw")
        s_D, s_E, s_Qt, s_Kt, s_lv, s_pred = (sem(n) for n in ("s_D", "s_E", "s_Qt", "s_Kt", "s_lv", "s_pred"))
        s_dgm, s_dg = sem("s_dgm"), sem("s_dg")
        s_dx, s_ex, s_kh, s_qh = sem("s_dx"), sem("s_ex"), sem("s_kh"), sem("s_qh")
        s_kt, s_ktc, s_ds, s_st, s_vb = sem("s_kt"), sem("s_ktc"), sem("s_ds"), sem("s_st"), sem("s_vb")
        s_dss, s_sn = sem("s_dss"), sem("s_sn")
        s_out, s_osb, s_osq, s_ost, s_rbo, s_or = (sem(n) for n in ("s_out", "s_osb", "s_osq", "s_ost", "s_rbo", "s_or"))
        s_mix = sem("s_mix")
        s_sq2, s_ahi, s_alo = sem("s_sq2"), sem("s_ahi"), sem("s_alo")
        s_xw, s_yt, s_yc = sem("s_xw"), sem("s_yt"), sem("s_yc")
        s_rbt = sem("s_rbt")
        s_y = [sem(f"s_y{i}") for i in range(TT + 1)]
        s_dve, s_act, s_pool = sem("s_dve"), sem("s_act"), sem("s_pool")

        def ordered(eng, own, start=None):
            seen = dict(start or {})

            def done(ins, s=None, by=1):
                s = own if s is None else s
                seen[s] = seen.get(s, 0) + by
                ins.then_inc(s, by)
                eng.wait_ge(s, seen[s])
            return done

        def pair_of(x):
            return PS[:, 2 * x.pair:2 * x.pair + 2, 0:HALF]

        def square(k):
            return tmp[k % 4] if k else rb

        def stats_bank(n):
            return 4 if n else 0

        def halves(ap):
            return ap.rearrange("p (a b) -> p a b", a=2)

        def split_index(n):
            return n % 2

        def weights(x, part, k, c0, cols=P):
            w = wR[split_index(x.split)]
            width = 512 if x.kind == "dn" else UC
            return w[:, part, k * width + c0:k * width + c0 + cols]

        def act_tile(x):
            n = 2 * x.i + x.n
            return (n // 4 % 2) * 4 + n % 4

        def raw_loads(u):
            return sum(64 if UNITS[v][0] == "q" else 16 for v in RING if v <= u and SLOT[v] == SLOT[u])

        def prompt_step(s):
            hp, n = divmod(s - SAMP, TT)
            return hp, n, hp // 2, (0, 1) if n else (1,)

        block = ctx.enter_context(nc.Block())

        @block.sync
        def _(sp):
            sp.dma_start(cn[:], a["c"]).then_inc(s_const, 16)
            sp.dma_start(vrow[:], a["vectors"]).then_inc(s_const, 16)
            sp.dma_start(ident[:], a["k_ident"]).then_inc(s_const, 16)

            def load(u):
                kind, i = UNITS[u]
                if u in BEFORE:
                    sp.wait_ge(s_lo, 4 * (SPLITS.index(BEFORE[u]) + 1))
                s = s_raw[SLOT[u]]
                dst = raw[SLOT[u]][:].rearrange("p (k c) -> p k c", c=UC)
                if kind == "q":
                    d = raw[SLOT[u]][:].rearrange("p (k j g c) -> p k j g c", j=2, g=2, c=HD)
                    for j in range(2):
                        for g in range(2):
                            h = (2 * (i // 2) + g) * GRP + 2 * (i % 2) + j
                            sp.dma_start(d[:, :, j, g, :], w_in[:, h * HD:(h + 1) * HD].rearrange("(k p) c -> p k c", p=P)).then_inc(s, 16)
                    return
                if kind == "dn":
                    g, half = divmod(i, 2)
                    src = a["w_down"][0][g * 512:(g + 1) * 512, half * 512:(half + 1) * 512]
                    dst = raw[SLOT[u]][:].rearrange("p (k c) -> p k c", c=512)
                elif kind == "out":
                    src = a["w_out"][0][:, i * UC:(i + 1) * UC]
                elif kind == "up":
                    src = a["w_up"][0][:, i * UC:(i + 1) * UC]
                else:
                    at = SEG[kind] + i * UC
                    src = w_in[:, at:at + UC]
                sp.dma_start(dst, src.rearrange("(k p) c -> p k c", p=P)).then_inc(s, 16)

            def front_loads():
                for i in range(TT):
                    sp.dma_start(xn[:, i, :], a["x_prompt"][0][i * P:(i + 1) * P, :]).then_inc(s_x, 16)
                sp.dma_start(xn[0:SMP, TT, :], a["x_sample"].rearrange("b t d -> (b t) d")).then_inc(s_x, 16)
                for u in range(FRONT):
                    at = UNITS[u][1] * UC
                    sp.dma_start(ada[u][:].rearrange("p (k c) -> p k c", c=UC),
                                 w_ada[:, at:at + UC].rearrange("(k p) c -> p k c", p=P)).then_inc(s_ada[u], 16)
                    if u == 1:
                        load(RING[0])
                load(RING[1])

            def load_mid(u):
                n = MID.index(u)
                sp.wait_ge(s_mm, LAST[MID[n - 1]] + 1 if n else FRONT)
                at = UNITS[u][1] * UC
                sp.dma_start(mid[:].rearrange("p (k c) -> p k c", c=UC), w_ada[:, at:at + UC].rearrange("(k p) c -> p k c", p=P)).then_inc(s_mid, 16)

            def cache_loads():
                sp.wait_ge(s_mm, FRONT)
                sp.wait_ge(s_hhi, KT)
                sp.dma_start(Kc[:], a["cache_win_k"][0].rearrange("b w h d -> w b (h d)")).then_inc(s_cache, 16)
                sp.dma_start(Vc[:], a["cache_win_v"][0].rearrange("b w h d -> w b (h d)")).then_inc(s_cache, 16)

            def table_loads():
                sp.dma_start(biasS[:], a["k_bias_s"]).then_inc(s_tables, 16)
                sp.dma_start(sink_s[:], a["sink_rows"]).then_inc(s_tables, 16)
                sp.dma_start(dist[:].rearrange("p a b -> p (a b)"), a["k_dist"]).then_inc(s_tables, 16)
                sp.dma_start(sink[:], a["attn_sinks"].to_broadcast([P, HEADS])).then_inc(s_tables, 16)
                sp.wait_ge(s_xr, KT)
                sp.dma_start(spill, xT[:].rearrange("p a b -> p (a b)")).then_inc(s_spill, 16)
                sp.dma_start(own_seq[:], a["k_own_seq"]).then_inc(s_tables, 16)
                sp.dma_start(resets_f[:], a["k_resets"]).then_inc(s_tables, 16)
                sp.dma_start(levels_f[:], a["k_levels"]).then_inc(s_tables, 16)

            for ev, *x in walk():
                if ev == "load":
                    load(x[0])
                elif ev == "load_mid":
                    load_mid(x[0])
                elif ev == "front":
                    front_loads()
                elif ev == "caches":
                    cache_loads()
                elif ev == "tables":
                    table_loads()
                elif ev == "win":
                    for name in ("k", "v"):
                        sp.dma_start(o[f"win_{name}_sample"][0][:, 0:WIN - NT], a[f"cache_win_{name}"][0][:, NT:WIN]).then_inc(s_store, 16)
                    sp.wait_ge(s_kw, 2)
                    sp.dma_start(o["win_k_prompt"][0][0].rearrange("w h d -> w (h d)"), probs[0][:, 0:KV * HD]).then_inc(s_win, 16)
                    sp.dma_start(o["win_v_prompt"][0][0].rearrange("w h d -> w (h d)"), V[:, TT - 1, :]).then_inc(s_win, 16)
                    for b in range(NB):
                        rows = slice(b * NT, (b + 1) * NT)
                        sp.dma_start(o["win_k_sample"][0][b, WIN - NT:WIN].rearrange("w h d -> w (h d)"), probs[1][rows, 0:KV * HD]).then_inc(s_win, 16)
                        sp.dma_start(o["win_v_sample"][0][b, WIN - NT:WIN].rearrange("w h d -> w (h d)"), V[rows, TT, :]).then_inc(s_win, 16)
                elif ev == "g_start":
                    r = x[0]
                    if r == 0:
                        sp.wait_ge(s_win, (2 + 2 * NB) * 16)
                        sp.wait_ge(s_otc, STEPS - PREP)
                        sp.wait_ge(s_mm, LAST[MID[-1]] + 1)
                    else:
                        sp.wait_ge(s_out, r)
                        sp.wait_ge(s_sn, 2 * r)
                    sp.dma_start(S0[:], a["state_hgrn"][0][:, r].rearrange("b k v -> k b v")).then_inc(s_s0, 16)
                elif ev == "g_norm":
                    r = x[0]
                    sp.wait_ge(s_sn, 2 * (r + 1))
                    sp.wait_ge(s_st, r + 1)
                    sp.dma_start(o["hgrn_sample"][0][:, r].rearrange("b k v -> k b v"), S1[:]).then_inc(s_state_out, 16)
                    sp.dma_start(o["hgrn_prompt"][0][0, r], S[:, TT - 1, :]).then_inc(s_state_out, 16)
                elif ev == "evac" and x[0].kind == "rg" and x[0].t == LAST[x[0].u] and x[0].i == 3:
                    sp.wait_ge(s_mix, 2 * RH)
                    sp.wait_ge(s_spill, 16)
                    sp.dma_start(xT[:].rearrange("p a b -> p (a b)"), spill).then_inc(s_back, 16)
                    sp.wait_ge(s_or, RH)
                    sp.wait_ge(s_state_out, 32 * RH)
                    for i, u in enumerate(LATE):
                        at = UNITS[u][1] * UC
                        sp.dma_start(late[i][:].rearrange("p (k c) -> p k c", c=UC),
                                     w_ada[:, at:at + UC].rearrange("(k p) c -> p k c", p=P)).then_inc(s_late[i], 16)
                elif ev == "final":
                    for i in range(TT):
                        sp.wait_ge(s_y[i], 1)
                        sp.dma_start(o["y_prompt"][0][i * P:(i + 1) * P, :], ysb[:, i, :]).then_inc(s_store, 16)
                    sp.wait_ge(s_y[TT], 1)
                    sp.dma_start(o["y_sample"].rearrange("b t d -> (b t) d"), ysb[0:SMP, TT, :]).then_inc(s_store, 16)
            sp.wait_ge(s_store, (2 + TT + 1) * 16)
            sp.wait_ge(s_state_out, 32 * RH)
            sp.wait_ge(s_win, (2 + 2 * NB) * 16)

        @block.tensor
        def _(pe):
            state = {"stat": 0}

            def front():
                pe.wait_ge(s_const, 3 * 16)
                pe.transpose(PS[:, 0, 0:NVEC], vrow[:, :], ident[0:NVEC, 0:NVEC]).then_inc(s_pe_front, 1)
                pe.wait_ge(s_dve_front, 1)
                for k in range(KT):
                    mm = pe.transpose(PS[:, 1, k * NSEQ:(k + 1) * NSEQ], cn[:, k * P:(k + 1) * P], ident[0:NSEQ, 0:NSEQ])
                mm.then_inc(s_pe_front, 1)
                pe.wait_ge(s_x, (TT + 1) * 16)
                pe.wait_ge(s_dve_front, 3)
                for k in range(KT):
                    mm = pe.transpose(PS[:, 2, k * SMP:(k + 1) * SMP], xn[0:SMP, TT, k * P:(k + 1) * P], ident[0:SMP, 0:SMP])
                mm.then_inc(s_pe_front, 1)
                for k in range(KT):
                    bank = (3 + k) % 8
                    if k == KT - 1:
                        pe.wait_ge(s_xe, 1)
                    for i in range(TT):
                        mm = pe.transpose(PS[:, bank, i * P:(i + 1) * P], xn[:, i, k * P:(k + 1) * P], ident[:])
                    mm.then_inc(s_pe_front, 1)
                pe.wait_ge(s_xe, KT + 1)

            def stats(n):
                pe.wait_ge(s_acc, (n + 1) * SUMMED)
                if n == 2:
                    for k, src in [(0, rb)] + [(k, square(k)) for k in range(SUMMED + 1, KT)]:
                        if k:
                            pe.wait_ge(s_sq, n * KT + k + 1)
                        for i in range(TT + 1):
                            rows = P if i < TT else SMP
                            mm = pe.matmul(A[0][0:rows, i:i + 1], src[:, i * P:i * P + rows], ones[:, 0:1],
                                           start=(k == 0 and i == 0), stop=(k == KT - 1), skip_group_check=True)
                    mm.then_inc(s_stat, 1)
                    return
                for k, src in [(0, rb)] + [(k, square(k)) for k in range(SUMMED + 1, KT)]:
                    if k:
                        pe.wait_ge(s_sq, n * KT + k + 1)
                    for h in range(2):
                        mm = pe.matmul(PS[:, stats_bank(n) + h, 0:HALF], ones[:], src[:, h * HALF:(h + 1) * HALF], start=(k == 0), stop=(k == KT - 1))
                mm.then_inc(s_stat, 1)

            def tile_part(x, c):
                b0_, b1_ = 2 * x.pair, 2 * x.pair + 1
                if c == 0:
                    if x.t >= 2 and x.u != FRONT:
                        y = TILES[x.t - 2]
                        reader = READER[y.kind]
                        pe.wait_ge(dict(act=s_act_free, dve=s_dve_free, tanh=s_tused)[reader], count_read(y.t, reader))
                    if x.kind == "ada" and x.u < FRONT:
                        pe.wait_ge(s_ada[x.u], 16)
                    elif x.u in LATE:
                        pe.wait_ge(s_late[LATE.index(x.u)], 16)
                    elif x.kind == "ada":
                        pe.wait_ge(s_mid, 16 * (MID.index(x.u) + 1))
                    elif x.n == 0:
                        pe.wait_ge(s_lo, 4 * (x.split + 1))
                if x.kind == "ada":
                    w = ada[x.u] if x.u < FRONT else late[LATE.index(x.u)] if x.u in LATE else mid
                    for k in range(KT):
                        rows = slice(k % 4 * CG, (k % 4 + 1) * CG)
                        mm = pe.matmul(PS[rows, b0_, 0:UC], cT[:, k, :], w[:, k * UC:(k + 1) * UC], start=(k < 4), stop=(k >= 4))
                    mm.then_inc(s_mm, 1)
                    return
                if x.kind in ("v", "ri"):
                    for k in range(4 * c, 4 * c + 4):
                        lhs = [hR[:, part, k * TOK + x.n * P:k * TOK + (x.n + 1) * P] for part in range(2)]
                        for n, (l, w) in enumerate(((0, 0), (0, 1), (1, 0))):
                            mm = pe.matmul(PS[:, b0_, 0:UC], lhs[l], weights(x, w, k, 0, UC),
                                           start=(k == 0 and n == 0), stop=(k == KT - 1 and n == 2))
                    if c == 1:
                        mm.then_inc(s_mm, 1)
                    return
                if (x.kind, x.i) in JOINT:
                    if x.n:
                        return
                    if c == 0 and x.u != FRONT:
                        y = TILES[x.t - 1]
                        pe.wait_ge(dict(act=s_act_free, dve=s_dve_free, tanh=s_tused)[READER[y.kind]], count_read(y.t, READER[y.kind]))
                    for k in (2 * c, 2 * c + 1):
                        pe.wait_ge(s_hlo, (KT if x.kind == "up" else 0) + k + 1)
                        for m in range(2):
                            for h in range(2):
                                for n, (w, r) in enumerate(((0, 0), (0, 1), (1, 0))):
                                    rhs = hR[:, r, k * TOK + h * HALF:k * TOK + (h + 1) * HALF]
                                    mm = pe.matmul(PS[:, 2 * ((x.pair + m) % 2) + h, 0:HALF], weights(x, w, k, m * P), rhs,
                                                   start=(k == 0 and n == 0), stop=(k == KT - 1 and n == 2))
                    if c == 3:
                        mm.then_inc(s_mm, 2)
                    return
                if x.kind == "dn":
                    h, ks, col = c, range(4), x.n * P
                else:
                    h, ks, col = c // 2, range(4 * (c % 2), 4 * (c % 2) + 4), x.n * P
                last = KT - 1 if x.kind != "dn" else 3
                for k in ks:
                    if x.kind == "dn":
                        slot_ = (x.i // 2 % 2) * 4 + k
                        if x.n == 0 and h == 0 and x.i % 2 == 0:
                            pe.wait_ge(s_alo, 4 * (x.i // 2) + k + 1)
                        rhs = [actR[:, slot_, part, h * HALF:(h + 1) * HALF] for part in range(2)]
                    elif x.kind == "out":
                        if x.i == 0 and x.n == 0 and h == 0:
                            pe.wait_ge(s_mix, 2 * k + 2)
                        rhs = [actR[:, k, part, h * HALF:(h + 1) * HALF] for part in range(2)]
                    else:
                        rhs = [hR[:, part, k * TOK + h * HALF:k * TOK + (h + 1) * HALF] for part in range(2)]
                    for n, (w, r) in enumerate(((0, 0), (0, 1), (1, 0))):
                        mm = pe.matmul(PS[:, 2 * x.pair + h, 0:HALF], weights(x, w, k, col), rhs[r],
                                       start=(k == 0 and n == 0), stop=(k == last and n == 2))
                if c == CHUNKS.get(x.kind, 4) - 1:
                    mm.then_inc(s_mm, 1)

            def ada_sum(x):
                n = ADA.index(x.u)
                pe.wait_ge(s_part, n + 1)
                for m in range(2):
                    mm = pe.matmul(PS[:, 2 * x.pair + 1, m * NSEQ:(m + 1) * NSEQ], part[n % 2][:, m * P:(m + 1) * P], collect[:], start=True, stop=True)
                mm.then_inc(s_asum, 1)

            def a_score(s):
                if s >= 1:
                    pe.wait_ge(s_max, s)
                if s < PREP:
                    if s == 0:
                        pe.wait_ge(s_cache, 2 * 16)
                        pe.wait_ge(s_dve_free, FRONT)
                    for i in range(2):
                        for T in range(2):
                            mm = pe.transpose(A[0][:, (2 * i + T) * P:(2 * i + T + 1) * P], Kc[:, 2 * s + i, T * P:(T + 1) * P], ident[:])
                    mm.then_inc(s_score, 1)
                    return
                if s < SAMP:
                    b = s - PREP
                    if b == 0:
                        pe.wait_ge(s_qb, HEADS)
                    for T in range(2):
                        pe.matmul(A[0][:, 0:P], Qblk[:, T, b, :], KcT[:, b, T, :], start=(T == 0), stop=(T == 1))
                    for T in range(2):
                        mm = pe.matmul(A[0][:, P:P + SMP], Qblk[:, T, b, :], kT[:, T, SEQ:TOK], start=(T == 0), stop=(T == 1))
                    mm.then_inc(s_score, 1)
                    return
                hp, n, g, kts = prompt_step(s)
                rows = slice((g % 2) * HD, (g % 2 + 1) * HD)
                for e in range(2):
                    j = 2 * (hp % 2) + e
                    q = qT[rows, (g // 2) * GRP + j, n * P:(n + 1) * P]
                    k0 = (n - 1 + kts[0]) * P
                    mm = pe.matmul(A[0][:, e * 2 * P + kts[0] * P:(e + 1) * 2 * P], q, kT[rows, g // 2, k0:(n + 1) * P], start=True, stop=True)
                mm.then_inc(s_score, 1)

            def a_probs(s):
                pe.wait_ge(s_exp, s - PREP + 1)
                if s > PREP:
                    pe.wait_ge(s_ptc, s - PREP)
                p = probs[s % 2]
                if s < SAMP:
                    pe.transpose(A[1][:, 0:P], p[:, 0:P], ident[:])
                    mm = pe.transpose(A[1][0:SMP, P:2 * P], p[:, P:P + SMP], ident[:])
                else:
                    for kt in prompt_step(s)[3]:
                        for e in range(2):
                            mm = pe.transpose(A[1][:, (2 * kt + e) * P:(2 * kt + e + 1) * P], p[:, (2 * e + kt) * P:(2 * e + kt + 1) * P], ident[:])
                mm.then_inc(s_pt, 1)

            def a_value(s):
                pe.wait_ge(s_ptc, s - PREP + 1)
                if s > PREP:
                    pe.wait_ge(s_o, s - PREP)
                if s < SAMP:
                    b = s - PREP
                    pe.matmul(A[2][:, 0:KV * HD], probsT[:, 0:P], Vc[:, b, :], start=True, stop=False)
                    mm = pe.matmul(A[2][:, 0:KV * HD], probsT[0:SMP, P:2 * P], V[0:SMP, TT, :], start=False, stop=True)
                else:
                    hp, n, g, kts = prompt_step(s)
                    for e in range(2):
                        for kt in kts:
                            mm = pe.matmul(A[2][:, e * HD:(e + 1) * HD], probsT[:, (2 * kt + e) * P:(2 * kt + e + 1) * P],
                                           V[:, n - 1 + kt, g * HD:(g + 1) * HD], start=(kt == kts[0]), stop=(kt == 1))
                mm.then_inc(s_pv, 1)

            def a_turn(s):
                pe.wait_ge(s_o, s - PREP + 1)
                if s > PREP:
                    pe.wait_ge(s_otc, s - PREP)
                if s < SAMP:
                    mm = pe.transpose(A[3][0:HD, 0:P], osb[:, 0:HD], ident[:])
                else:
                    mm = pe.transpose(A[3][:, 0:P], osb[:, 0:P], ident[:])
                mm.then_inc(s_ot, 1)

            def win():
                pe.wait_ge(s_max, STEPS)
                for T in range(2):
                    pe.transpose(A[0][:, T * P:(T + 1) * P], kT[:, T, SEQ - P:SEQ], ident[:])
                for T in range(2):
                    mm = pe.transpose(A[0][0:SMP, (2 + T) * P:(3 + T) * P], kT[:, T, SEQ:TOK], ident[:])
                mm.then_inc(s_score, 1)

            def g_diag(r):
                k, q = KR[r // 2 % 2], QS[r // 2 % 2]
                pe.wait_ge(s_tused, TANH.index(LAST[UNITS.index(("rq", r // 2))]) + 1)
                pe.wait_ge(s_otc, STEPS - PREP)
                if r:
                    pe.wait_ge(s_sn, 2 * r)
                for c in range(TT):
                    cols = slice(c * P, (c + 1) * P)
                    pe.matmul(A[2][:, cols], k[:, r % 2, cols], q[:, r % 2, cols], start=True, stop=True)
                pe.matmul(A[3][0:SMP, 0:SMP], k[:, r % 2, SEQ:TOK], q[:, r % 2, SEQ:TOK], start=True, stop=True).then_inc(s_dgm, 1)

            def g_level(r, l):
                n = r * NL + l
                pe.wait_ge(s_Qt, n + 1)
                pe.wait_ge(s_Kt, n + 1)
                if n >= 2:
                    pe.wait_ge(s_pred, n - 1)
                if l < 2 and r:
                    pe.wait_ge(s_rbo, r)
                elif l < 2:
                    pe.wait_ge(s_kw, 2)
                bank, q, k = A[l % 2], QTL[n % 2], KTL[n % 2]
                for c in range(TT):
                    mm = pe.matmul(bank[:, c * HD:(c + 1) * HD], k[:, c * P:(c + 1) * P], q[:, c * HD:(c + 1) * HD], start=True, stop=True)
                if LEVELS[l] < NT:
                    mm = pe.matmul(bank[:, SEQ // 2:HALF], k[:, SEQ:TOK + SMP], q[:, SEQ // 2:HALF], start=True, stop=True)
                mm.then_inc(s_lv, 1)

            def g_keys(r):
                pe.wait_ge(s_kh, r + 1)
                pe.wait_ge(s_dg, r + 1)
                for c in range(TT):
                    pe.transpose(A[2][:, c * P:(c + 1) * P], kh[:, c * P:(c + 1) * P], ident[:])
                pe.transpose(A[3][0:SMP, 0:P], kh[:, SEQ:TOK], ident[:]).then_inc(s_kt, 1)

            def g_state(r):
                pe.wait_ge(s_ktc, 2 * r + 2)
                v = RV[r // 2 % 2]
                e = (r % 2) * P
                for c in range(TT):
                    mm = pe.matmul(A[2][:, c * P:(c + 1) * P], khT[:, c, :], v[:, c, e:e + P], start=True, stop=True)
                mm.then_inc(s_ds, 1)

            def g_sample(r, h):
                pe.wait_ge(s_vb, r + 1)
                pe.wait_ge(s_ktc, 2 * r + 2)
                if h:
                    pe.wait_ge(s_st, r + 1)
                pe.matmul(A[3 - h][:, :], khT[0:SMP, TT, :], vblk[:, 4 * h:4 * h + 4, :].rearrange("p b v -> p (b v)"),
                          start=True, stop=True).then_inc(s_dss, 1)

            def g_out(r):
                v, e = RV[r // 2 % 2], (r % 2) * P
                pe.wait_ge(s_pred, (r + 1) * NL)
                pe.wait_ge(s_qh, r + 1)
                pe.wait_ge(s_st, r + 1)
                pe.wait_ge(s_s0, 16 * (r + 1))
                for c in range(TT):
                    cols = slice(c * P, (c + 1) * P)
                    if c:
                        pe.matmul(A[0][:, cols], S[:, c - 1, :], qh[:, cols], start=True, stop=False)
                    pe.matmul(A[0][:, cols], v[:, c, e:e + P], att[:, cols], start=(c == 0), stop=True)
                pe.matmul(A[1][:, 0:SMP], v[0:SMP, TT, e:e + P], att[0:SMP, SEQ:TOK], start=True, stop=False, skip_group_check=True)
                for b in range(NB):
                    mm = pe.matmul(A[1][:, b * NT:(b + 1) * NT], S0[:, b, :], qh[:, SEQ + b * NT:SEQ + (b + 1) * NT],
                                   start=False, stop=(b == NB - 1), skip_group_check=True)
                mm.then_inc(s_out, 1)

            def g_norm(r):
                pe.wait_ge(s_osq, r + 1)
                for h in range(2):
                    mm = pe.matmul(A[h][:, 0:HALF], ones[:], att[:, h * HALF:(h + 1) * HALF], start=True, stop=True)
                mm.then_inc(s_ost, 1)

            def y_turn(k):
                pe.wait_ge(s_xw, k + 1)
                if k:
                    pe.wait_ge(s_yc, 2 * k)
                for i in range(TT):
                    pe.transpose(A[1 + k % 2][:, i * P:(i + 1) * P], xw[:, k, i * P:(i + 1) * P], ident[:])
                pe.transpose(A[3][0:SMP, 0:P], xw[:, k, SEQ:TOK], ident[:]).then_inc(s_yt, 1)

            for ev, *x in walk():
                if ev == "front":
                    front()
                elif ev == "norm":
                    stats(0)
                elif ev == "finish_stats":
                    stats(*x)
                elif ev == "mm":
                    tile_part(*x)
                elif ev == "ada_sum":
                    ada_sum(*x)
                elif ev == "a_score":
                    a_score(*x)
                elif ev == "a_probs":
                    a_probs(*x)
                elif ev == "a_value":
                    a_value(*x)
                elif ev == "a_turn":
                    a_turn(*x)
                elif ev == "win":
                    win()
                elif ev == "g_diag":
                    g_diag(*x)
                elif ev == "g_level":
                    g_level(*x)
                elif ev == "g_keys":
                    g_keys(*x)
                elif ev == "g_state":
                    g_state(*x)
                elif ev == "g_sample":
                    g_sample(*x)
                elif ev == "g_out":
                    g_out(*x)
                elif ev == "g_norm":
                    g_norm(*x)
                elif ev == "y_turn":
                    y_turn(*x)

        @block.scalar
        def _(act):
            done = ordered(act, s_act)
            seen = {"tanh": 0}

            def front():
                act.wait_ge(s_const, 3 * 16)
                done(act.activation(cgate[:], cn[:], ACT.Tanh, scale=0.5), s_act_front)
                act.wait_ge(s_dve_front, 4)
                done(act.activation(lb[:], lb[:], ACT.Exp), s_act_front)
                for k in range(KT):
                    act.wait_ge(s_xe, k + 2)
                    squares(0, k)

            def squares(n, k):
                if k > SUMMED:
                    act.wait_ge(s_acc, n * SUMMED + k - 4)
                if n:
                    act.wait_ge(s_x2, (n - 1) * KT + k + 1)
                if k == KT - 1:
                    act.preload_act_table(ACT.Ln)
                done(act.activation(square(k)[:], xT[:, k, :], ACT.Square), s_sq)
                if n == 2:
                    done(act.activation(xw[:, k, :], xT[:, k, :], ACT.Copy, scale=vec[:, VN["fin"] + k:VN["fin"] + k + 1]), s_xw)

            def rms(bank, size, signal):
                for h in range(2):
                    done(act.activation(rb[:, h * HALF:(h + 1) * HALF], PS[:, bank + h, 0:HALF], ACT.Ln, scale=1.0 / size, bias=eps[:, 0:1]))
                done(act.activation(rb[:], rb[:], ACT.Exp, scale=-0.5), signal)

            def norm(n):
                act.wait_ge(s_stat, n + 1)
                if n == 2:
                    parts = [(slice(0, P), slice(0, TT)), (slice(0, SMP), slice(TT, TT + 1))]
                    for rows, cols in parts:
                        done(act.activation(rbt[rows, cols], A[0][rows, cols], ACT.Ln, scale=1.0 / DM, bias=eps[rows, 0:1]))
                    for rows, cols in parts:
                        done(act.activation(rbt[rows, cols], rbt[rows, cols], ACT.Exp, scale=-0.5), s_rbt)
                    return
                rms(stats_bank(n), DM, s_rb)

            def g_norm(r):
                act.wait_ge(s_ost, r + 1)
                if r:
                    act.wait_ge(s_or, r)
                rms(4, P, s_rbo)

            def modulate(n, k0):
                sh, sc = (0, KT) if n == 0 else (3 * KT, 4 * KT)
                for k in (k0, k0 + 1):
                    act.wait_ge(s_xr, n * KT + k + 1)
                    act.wait_ge(s_vec, n * KT // 2 + k0 // 2 + 1)
                    if k >= 4:
                        act.wait_ge(s_hlo, n * KT + k - 3)
                    h = tmp[k % 4]
                    done(act.activation(h[:, 0:SEQ], xhat[n][:, k, 0:SEQ], ACT.Identity, scale=mods[:, sc + k, 0:1], bias=mods[:, sh + k, 0:1]))
                    act.wait_ge(s_hs, n * KT + k + 1)
                    done(act.activation(hR[:, 0, k * TOK:(k + 1) * TOK], h[:], ACT.Copy), s_hhi)

            def evac(x):
                src = pair_of(x)
                if READER[x.kind] == "dve":
                    return
                act.wait_ge(s_mm, x.t + 1)
                if x.kind in ("k", "q"):
                    dst = kT[:, x.n, :] if x.kind == "k" else qT[:, 2 * x.i + x.n, :]
                    done(act.activation(halves(dst), src, ACT.Copy), s_act_free)
                elif x.kind in ("v", "ri"):
                    rows = P if x.n < TT else SMP
                    dst = V if x.kind == "v" else RV[x.i % 2]
                    done(act.activation(dst[0:rows, x.n, :], PS[0:rows, 2 * x.pair, 0:UC], ACT.Copy), s_act_free)
                elif x.kind == "rf":
                    n = 2 * x.i + x.n
                    if n == 0:
                        act.wait_ge(s_hlo, KT)
                    if n >= 2:
                        act.wait_ge(s_scan, n - 1)
                    done(act.activation(halves(tmp[x.n][:]), src, ACT.Sigmoid), s_act_free)
                    if x.n == 1:
                        for e in range(2):
                            r = 2 * x.i + e
                            act.wait_ge(s_clamp, r + 1)
                            done(act.activation(tmp[e][:], tmp[e][:], ACT.Ln, scale=omlb[:, r:r + 1], bias=lb[:, r:r + 1]), s_ln)
                elif x.kind in ("rq", "ga", "gr", "rg"):
                    n = seen["tanh"]
                    seen["tanh"] += 1
                    if n >= 2:
                        act.wait_ge(s_tused, n - 1)
                    s = s_act_free if x.kind in ("ga", "gr") else s_tanh
                    done(act.activation(halves(tmp[2 + n % 2][:]), src, ACT.Tanh, scale=0.5), s)
                elif x.kind == "up":
                    n = 2 * x.i + x.n
                    if n >= 2:
                        act.wait_ge(s_alo, n - 1)
                    t = tmp[n % 2][:]
                    done(act.activation(halves(t), src, ACT.Relu), s_act_free)
                    done(act.activation(t, t, ACT.Square), s_sq2)

            def a_exp(s):
                q = s - PREP
                act.wait_ge(s_neg, q + 1)
                m, p = small[:, s % 4], probs[s % 2]
                if s < SAMP:
                    done(act.activation(p[:, 0:P + SMP], p[:, 0:P + SMP], ACT.Exp, bias=m[:, 1, 0:1], accum_out=m[:, 3, 0:1]))
                    done(act.activation(m[:, 2, 0:1], m[:, 2, 0:1], ACT.Exp), s_exp)
                    return
                k0 = prompt_step(s)[3][0] * P
                for e in range(2):
                    t = p[:, e * 2 * P + k0:(e + 1) * 2 * P]
                    done(act.activation(t, t, ACT.Exp, bias=m[:, 1, e:e + 1], accum_out=m[:, 3, e:e + 1]))
                done(act.activation(m[:, 2, :], m[:, 2, :], ACT.Exp), s_exp)

            def a_take(s):
                act.wait_ge(s_pt, s - PREP + 1)
                if s > PREP:
                    act.wait_ge(s_pv, s - PREP)
                if s < SAMP:
                    done(act.activation(probsT[:, 0:P], A[1][:, 0:P], ACT.Copy))
                    done(act.activation(probsT[0:SMP, P:2 * P], A[1][0:SMP, P:2 * P], ACT.Copy), s_ptc)
                    return
                k0 = prompt_step(s)[3][0] * 2 * P
                done(act.activation(probsT[:, k0:4 * P], A[1][:, k0:4 * P], ACT.Copy), s_ptc)

            def a_put(s):
                act.wait_ge(s_ot, s - PREP + 1)
                if s == PREP:
                    act.wait_ge(s_spill, 16)
                if s < SAMP:
                    b = s - PREP
                    src = A[3][0:HD, 0:P].rearrange("p (k e t) -> p k e t", e=2, t=NT)
                    cols = slice(SEQ + b * NT, SEQ + (b + 1) * NT)
                    done(act.activation(attnT[0:HD, :, cols], src[:, :, 0, :], ACT.Copy))
                    done(act.activation(attnT[HD:P, :, cols], src[:, :, 1, :], ACT.Copy), s_otc)
                    return
                hp, n, g, kts = prompt_step(s)
                done(act.activation(attnT[:, hp, n * P:(n + 1) * P], A[3][:, 0:P], ACT.Copy), s_otc)

            def g_exp(r, l):
                m, i = LEVELS[l], r * NL + l
                n = TOK if m < NT else SEQ
                act.wait_ge(s_D, i + 1)
                d = D[i % 3][:, 0:n].rearrange("p (a m) -> p a m", m=2 * m)
                done(act.activation(d[:, :, m:2 * m], d[:, :, m:2 * m], ACT.Exp))
                done(act.activation(d[:, :, 0:m], d[:, :, 0:m], ACT.Exp, scale=-1.0), s_E)

            def g_hats(r):
                if r:
                    act.wait_ge(s_sn, 2 * r)
                done(act.activation(eb[:], B[r // 2 % 2][:, r % 2, :], ACT.Exp))
                act.wait_ge(s_dx, r + 1)
                done(act.activation(kh[:], kh[:], ACT.Exp), s_ex)

            def g_keys(r):
                act.wait_ge(s_kt, r + 1)
                if r == 0:
                    act.wait_ge(s_win, (2 + 2 * NB) * 16)
                done(act.activation(khT[:, 0:TT, :], A[2].rearrange("p (c k) -> p c k", k=P), ACT.Copy), s_ktc)
                done(act.activation(khT[0:SMP, TT, :], A[3][0:SMP, 0:P], ACT.Copy), s_ktc)

            def g_out(r):
                act.preload_act_table(ACT.Ln)
                act.wait_ge(s_out, r + 1)
                done(act.activation(osc[:, 0:SEQ], A[0][:, :], ACT.Copy, scale=QSCALE))
                done(act.activation(osc[:, SEQ:TOK], A[1][:, 0:SMP], ACT.Copy, scale=QSCALE), s_osb)
                done(act.activation(att[:], osc[:], ACT.Square), s_osq)

            def final():
                act.wait_ge(s_yc, 2 * KT)
                for i in (1, 3):
                    done(act.activation(ysb[:, i, :], ysb[:, i, :], ACT.Copy, scale=rbt[:, i:i + 1]), s_y[i])

            for ev, *x in walk():
                if ev == "front":
                    front()
                elif ev == "norm":
                    norm(0)
                elif ev == "finish_stats":
                    norm(*x)
                elif ev == "g_norm":
                    g_norm(*x)
                elif ev == "stats":
                    squares(*x)
                elif ev == "modulate":
                    modulate(*x)
                elif ev == "evac":
                    evac(*x)
                elif ev == "a_exp":
                    a_exp(*x)
                elif ev == "a_take":
                    a_take(*x)
                elif ev == "a_put":
                    a_put(*x)
                elif ev == "g_exp":
                    g_exp(*x)
                elif ev == "g_hats":
                    g_hats(*x)
                elif ev == "g_keys":
                    g_keys(*x)
                elif ev == "g_out":
                    g_out(*x)
                elif ev == "final":
                    final()

        @block.vector
        def _(dve):
            done = ordered(dve, s_dve)
            seen = {"tanh": 0}

            def per_seq(ap):
                return ap.rearrange("p (b t) -> p b t", t=NT)

            def mod_s(k):
                return mods[:, k, 1:NSEQ].unsqueeze(2).to_broadcast([P, NB, NT])

            def front():
                done(dve.memset(ones[:], 1.0))
                done(dve.memset(eps[:], EPS))
                done(dve.memset(hR[:, :, KT * TOK:].bitcast(F32), 0.0))
                done(dve.memset(cT[:], 0.0))
                dve.wait_ge(s_act_front, 1)
                done(dve.scalar_tensor_tensor(cn[:], cgate[:], 1.0, cn[:], ALU.add, ALU.mult))
                done(dve.tensor_scalar(cn[:], cn[:], 0.5, None, ALU.mult), s_dve_front)
                dve.wait_ge(s_pe_front, 1)
                done(dve.tensor_copy(vec[:], PS[:, 0, 0:NVEC]), s_dve_front)
                dve.wait_ge(s_pe_front, 2)
                done(dve.tensor_copy(cT[:, :, 0:NSEQ], PS[:, 1, 0:KT * NSEQ].rearrange("p (k c) -> p k c", c=NSEQ)), s_dve_front)
                lo = vec[:, VN["lb"]:VN["lb"] + KT]
                done(dve.tensor_tensor(lb[:], lo, lo, ALU.subtract), s_dve_front)
                dve.wait_ge(s_pe_front, 3)
                done(dve.tensor_copy(xT[:, :, SEQ:TOK], PS[:, 2, :].rearrange("p (k t) -> p k t", t=SMP)), s_xe)
                for k in range(KT):
                    dve.wait_ge(s_pe_front, 4 + k)
                    done(dve.tensor_copy(xT[:, k, 0:SEQ], PS[:, (3 + k) % 8, :]), s_xe)
                dve.wait_ge(s_act_front, 2)
                done(dve.reciprocal(omlb[:], lb[:]))
                done(dve.tensor_tensor(omlb[:], lb[:], omlb[:], ALU.mult))
                done(dve.tensor_tensor(lb[:], omlb[:], omlb[:], ALU.subtract))
                done(dve.tensor_scalar(omlb[:], lb[:], -1.0, 1.0, ALU.mult, ALU.add))
                done(dve.tensor_scalar(nomlb[:], omlb[:], -1.0, None, ALU.mult))
                done(dve.tensor_tensor(collect[:], ident[:, 0:NSEQ], ident[:, CG:CG + NSEQ], ALU.add))
                for j in (2, 3):
                    done(dve.tensor_tensor(collect[:], collect[:], ident[:, j * CG:j * CG + NSEQ], ALU.add))

            def masks():
                dve.wait_ge(s_tables, 7 * 16)
                done(dve.tensor_copy(resets[:], resets_f[:]))
                done(dve.tensor_copy(levels[:].rearrange("p a b -> p (a b)"), levels_f[:]))

            def ada_part(x):
                n = ADA.index(x.u)
                if n >= 2:
                    dve.wait_ge(s_asum, n - 1)
                dve.wait_ge(s_mm, x.t + 1)
                done(dve.tensor_copy(part[n % 2][:], PS[:, 2 * x.pair, 0:UC]), s_part)

            def scale_vectors(n, k0):
                sc, g = (KT, VN["mix"]) if n == 0 else (4 * KT, VN["mlp"])
                v = mods[:, sc + k0:sc + k0 + 2, :]
                done(dve.scalar_tensor_tensor(v, v, 1.0, vec[:, g + k0:g + k0 + 2].unsqueeze(2).to_broadcast([P, 2, NSEQ]), ALU.add, ALU.mult), s_vec)

            def modulate(n, k0):
                sh, sc = (0, KT) if n == 0 else (3 * KT, 4 * KT)

                def normalise(k):
                    if k < KT:
                        done(dve.tensor_tensor(xhat[n][:, k, :], xT[:, k, :], rb[:], ALU.mult), s_xr)

                if n == 0:
                    scale_vectors(0, k0)
                if k0 == 0:
                    dve.wait_ge(s_rb, n + 1)
                    if n:
                        dve.wait_ge(s_state_out, 32 * RH)
                        dve.wait_ge(s_mm, max(x.t for x in TILES if x.kind == "rg") + 1)
                    normalise(0)
                for k in (k0, k0 + 1):
                    if k >= 4:
                        dve.wait_ge(s_hlo, n * KT + k - 3)
                    hs = per_seq(tmp[k % 4][:, SEQ:TOK])
                    done(dve.tensor_tensor(hs, per_seq(xhat[n][:, k, SEQ:TOK]), mod_s(sc + k), ALU.mult))
                    done(dve.tensor_tensor(hs, hs, mod_s(sh + k), ALU.add), s_hs)
                    normalise(k + 1)

            def hi(n):
                u = SPLITS[n]
                dve.wait_ge(s_raw[SLOT[u]], raw_loads(u))
                if n >= 2:
                    dve.wait_ge(s_mm, LAST[SPLITS[n - 2]] + 1)
                done(dve.tensor_copy(wR[split_index(n)][:, 0, :], raw[SLOT[u]][:]), s_hi)

            def lo(n):
                w = wR[split_index(n)]
                done(dve.tensor_tensor(w[:, 1, :], raw[SLOT[SPLITS[n]]][:], w[:, 0, :].bitcast(F32), ALU.subtract), s_lo, 4)

            def residual(x, m, gate):
                b0_ = 2 * x.pair
                dve.wait_ge(s_mm, x.t + 1)
                cut = SEQ - HALF
                done(dve.scalar_tensor_tensor(xT[:, m, 0:HALF], PS[:, b0_, 0:HALF], mods[:, gate + m, 0:1], xT[:, m, 0:HALF], ALU.mult, ALU.add))
                done(dve.scalar_tensor_tensor(xT[:, m, HALF:SEQ], PS[:, b0_ + 1, 0:cut], mods[:, gate + m, 0:1], xT[:, m, HALF:SEQ], ALU.mult, ALU.add))
                done(dve.tensor_tensor(per_seq(tmp_s[:]), per_seq(PS[:, b0_ + 1, cut:HALF]), mod_s(gate + m), ALU.mult), s_dve_free)
                last = xT[:, m, SEQ:TOK]
                signal = x.kind == "out" or x.i >= 14
                done(dve.tensor_tensor(last, last, tmp_s[:], ALU.add), s_x2 if signal else None)

            def evac(x):
                if x.kind == "ada":
                    m = 2 * x.i
                    dve.wait_ge(s_asum, ADA.index(x.u) + 1)
                    done(dve.tensor_tensor(mods[:, m:m + 2, :], PS[:, 2 * x.pair + 1, 0:2 * NSEQ].rearrange("p (m c) -> p m c", c=NSEQ),
                                           vec[:, VN["bada"] + m:VN["bada"] + m + 2].unsqueeze(2).to_broadcast([P, 2, NSEQ]), ALU.add), s_dve_free)
                elif x.kind == "rf":
                    n, e = 2 * x.i + x.n, x.n
                    t = tmp[e]
                    dve.wait_ge(s_act_free, count_read(x.t, "act"))
                    done(dve.tensor_scalar(KR[x.i % 2][:, e, :], t[:], 1.0, nomlb[:, n:n + 1], ALU.subtract, ALU.mult))
                    done(dve.tensor_scalar(t[:], t[:], LEAST, None, ALU.max), s_clamp)
                elif x.kind in ("rq", "ga", "gr", "rg"):
                    n = seen["tanh"]
                    seen["tanh"] += 1
                    t = tmp[2 + n % 2]
                    if x.kind in ("ga", "gr"):
                        dve.wait_ge(s_act_free, count_read(x.t, "act"))
                    else:
                        dve.wait_ge(s_tanh, sum(TILES[y].kind in ("rq", "rg") for y in TANH[:n + 1]))
                    r = 2 * x.i + x.n
                    if x.kind == "rq":
                        done(dve.scalar_tensor_tensor(halves(QS[x.i % 2][:, x.n, :]), halves(t[:]), 1.0, pair_of(x), ALU.add, ALU.mult), s_tused)
                    elif x.kind == "ga":
                        dve.wait_ge(s_otc, SAMP - PREP + (r + 1) * TT)
                        done(dve.scalar_tensor_tensor(attnT[:, r, :], t[:], 1.0, attnT[:, r, :], ALU.add, ALU.mult), s_tused)
                    elif x.kind == "gr":
                        done(dve.scalar_tensor_tensor(orec[:, r, :], t[:], 1.0, orec[:, r, :], ALU.add, ALU.mult), s_tused)
                    else:
                        done(dve.scalar_tensor_tensor(halves(tmp[x.n][:]), halves(t[:]), 1.0, pair_of(x), ALU.add, ALU.mult), s_tused)
                elif x.kind == "up":
                    n = 2 * x.i + x.n
                    if n == 0:
                        dve.wait_ge(s_mm, max(y.t for y in TILES if y.kind == "out") + 1)
                    if n >= 8:
                        dve.wait_ge(s_mm, LAST[UNITS.index(("dn", 2 * (n // 4 - 2) + 1))] + 1)
                    dve.wait_ge(s_sq2, n + 1)
                    done(dve.tensor_copy(actR[:, act_tile(x), 0, :], tmp[n % 2][:]), s_ahi)
                elif x.kind == "out":
                    if x.i == 0 and x.n == 0:
                        dve.wait_ge(s_back, 16)
                    residual(x, 2 * x.i + x.n, 2 * KT)
                elif x.kind == "dn":
                    residual(x, 4 * (x.i % 2) + x.n, 5 * KT)

            def scan(i):
                for f in range(2):
                    dve.wait_ge(s_ln, 2 * i + f + 1)
                    done(dve.tensor_tensor_scan(B[i % 2][:, f, :], resets[:], tmp[f][:], 0.0, ALU.mult, ALU.add), s_scan)

            def q_blocks(i):
                if i == 0:
                    done(dve.memset(Qblk[:].rearrange("p a b c -> p (a b c)"), 0.0))
                dve.wait_ge(s_act_free, count_read(LAST[UNITS.index(("q", i))], "act"))
                for g in (i // 2 * 2, i // 2 * 2 + 1):
                    rows, T = slice((g % 2) * HD, (g % 2 + 1) * HD), g // 2
                    for j in (i % 2 * 2, i % 2 * 2 + 1):
                        c = g * GRP * NT + j * NT
                        src = per_seq(qT[rows, T * GRP + j, SEQ:TOK])
                        done(dve.tensor_copy(Qblk[rows, T, :, c:c + NT], src), s_qb)

            def a_max(s):
                dve.wait_ge(s_score, s + 1)
                if s < PREP:
                    done(dve.tensor_copy(KcT[:, 2 * s:2 * s + 2, :, :].rearrange("p b t w -> p (b t w)"), A[0]), s_max)
                    return
                if s - PREP >= 2:
                    dve.wait_ge(s_pt, s - PREP - 1)
                m, p = small[:, s % 4], probs[s % 2]
                if s < SAMP:
                    b = s - PREP
                    done(dve.tensor_tensor_reduce(p[:, 0:P], A[0][:, 0:P], biasS[:, 0:P], HD ** -0.5, sink_s[:, 0:1], ALU.add, ALU.max, m[:, 5, 0:1]))
                    new = biasS[:, P + 56 - b * NT:P + 56 - b * NT + SMP]
                    done(dve.tensor_tensor_reduce(p[:, P:P + SMP], A[0][:, P:P + SMP], new, HD ** -0.5, m[:, 5, 0:1], ALU.add, ALU.max, m[:, 0, 0:1]), s_max)
                    done(dve.tensor_tensor(m[:, 2, 0:1], sink_s[:, 0:1], m[:, 0, 0:1], ALU.subtract))
                    done(dve.tensor_scalar(m[:, 1, 0:1], m[:, 0, 0:1], -1.0, None, ALU.mult), s_neg)
                    return
                hp, n, g, kts = prompt_step(s)
                k0 = kts[0] * P
                if n == 0:
                    for e in range(2):
                        slope = 2.0 ** (-8.0 * (2 * hp + e + 1) / HEADS)
                        done(dve.scalar_tensor_tensor(biasP[:, e, :], dist[:, 0, :], -slope * HD ** 0.5, dist[:, 1, :], ALU.mult, ALU.add))
                for e in range(2):
                    cols = slice(e * 2 * P + k0, (e + 1) * 2 * P)
                    h = 2 * hp + e
                    done(dve.tensor_tensor_reduce(p[:, cols], A[0][:, cols], biasP[:, e, k0:2 * P], HD ** -0.5, sink[:, h:h + 1],
                                                  ALU.add, ALU.max, m[:, 0, e:e + 1]), s_max if e else None)
                done(dve.tensor_tensor(m[:, 2, :], sink[:, 2 * hp:2 * hp + 2], m[:, 0, :], ALU.subtract))
                done(dve.tensor_scalar(m[:, 1, :], m[:, 0, :], -1.0, None, ALU.mult), s_neg)

            def a_scale(s):
                m = small[:, s % 4]
                w = 1 if s < SAMP else 2
                dve.wait_ge(s_exp, s - PREP + 1)
                done(dve.tensor_tensor(m[:, 4, 0:w], m[:, 3, 0:w], m[:, 2, 0:w], ALU.add))
                done(dve.reciprocal(m[:, 4, 0:w], m[:, 4, 0:w]))
                dve.wait_ge(s_pv, s - PREP + 1)
                if s > PREP:
                    dve.wait_ge(s_ot, s - PREP)
                if s < SAMP:
                    for g in range(KV):
                        rows = slice(g * GRP * NT, (g + 1) * GRP * NT)
                        done(dve.tensor_scalar(osb[rows, 0:HD], A[2][rows, g * HD:(g + 1) * HD], m[rows, 4, 0:1], None, ALU.mult),
                             s_o if g == KV - 1 else None)
                    return
                done(dve.tensor_tensor(osb[:].rearrange("p (e d) -> p e d", e=2), A[2][:, 0:P].rearrange("p (e d) -> p e d", e=2),
                                       m[:, 4, :].unsqueeze(2).to_broadcast([P, 2, HD]), ALU.mult), s_o)

            def win():
                dve.wait_ge(s_score, STEPS + 1)
                dve.wait_ge(s_pt, STEPS - PREP)
                done(dve.tensor_copy(probs[0][:, 0:KV * HD], A[0][:, 0:KV * HD]), s_kw)
                done(dve.tensor_copy(probs[1][0:SMP, 0:KV * HD], A[0][0:SMP, KV * HD:2 * KV * HD]), s_kw)

            def merge(x, step):
                m, r = tmp[x.n], 2 * x.i + x.n
                if step == 0:
                    done(dve.tensor_tensor(m[:], m[:], orec[:, r, :], ALU.mult))
                    done(dve.scalar_tensor_tensor(m[:], m[:], 0.5, attnT[:, r, :], ALU.mult, ALU.add))
                else:
                    done(dve.tensor_scalar(actR[:, r, 0, :], m[:], 0.5, None, ALU.mult), s_mix)
                    done(dve.scalar_tensor_tensor(actR[:, r, 1, :], m[:], 0.5, actR[:, r, 0, :].bitcast(F32), ALU.mult, ALU.subtract), s_mix)

            def g_operands(r, l):
                m, n = LEVELS[l], r * NL + l
                w = TOK if m < NT else SEQ
                view = lambda t: t[:, 0:w].rearrange("p (a m) -> p a m", m=2 * m)
                q, k = QS[r // 2 % 2][:, r % 2, :], KR[r // 2 % 2][:, r % 2, :]
                d = view(D[n % 3])
                if n < 2:
                    if n == 0:
                        dve.wait_ge(s_score, STEPS + 1)
                    done(dve.memset(KTL[n % 2][:], 0.0))
                dve.wait_ge(s_E, n + 1)
                if n >= 2:
                    dve.wait_ge(s_lv, n - 1)
                done(dve.tensor_tensor(QTL[n % 2][:, 0:w // 2].rearrange("p (a m) -> p a m", m=m), view(q)[:, :, m:2 * m], d[:, :, m:2 * m], ALU.mult), s_Qt)
                done(dve.tensor_tensor(view(KTL[n % 2])[:, :, 0:m], view(k)[:, :, 0:m], d[:, :, 0:m], ALU.mult), s_Kt)

            def g_diag(r):
                dve.wait_ge(s_dgm, r + 1)
                if r:
                    dve.wait_ge(s_ost, r)
                done(dve.tensor_tensor(att[:, 0:SEQ].rearrange("p (c t) -> p c t", t=P), A[2].rearrange("p (c t) -> p c t", t=P),
                                       ident[:].unsqueeze(1).to_broadcast([P, TT, P]), ALU.mult))
                if r == 0:
                    done(dve.memset(att[SMP:P, SEQ:TOK], 0.0))
                done(dve.tensor_tensor(att[0:SMP, SEQ:TOK], A[3][0:SMP, 0:SMP], ident[0:SMP, 0:SMP], ALU.mult), s_dg)

            def g_level(r, l):
                m, n = LEVELS[l], r * NL + l
                w = TOK if m < NT else SEQ
                dve.wait_ge(s_lv, n + 1)
                half = lambda t: t[:, 0:w // 2].rearrange("p (a m) -> p a m", m=m)
                done(dve.copy_predicated(att[:, 0:w].rearrange("p (a m) -> p a m", m=2 * m)[:, :, m:2 * m], half(levels[:, l, :]), half(A[l % 2])), s_pred)

            def g_products(r):
                dve.wait_ge(s_ex, r + 1)
                done(dve.tensor_tensor(kh[:], KR[r // 2 % 2][:, r % 2, :], kh[:], ALU.mult), s_kh)

            def g_keys(r):
                e = (r % 2) * P
                if r:
                    dve.wait_ge(s_dss, 2 * r)
                else:
                    dve.wait_ge(s_win, (2 + 2 * NB) * 16)
                done(dve.tensor_tensor(vblk[:], RV[r // 2 % 2][0:SMP, TT, e:e + P].unsqueeze(1).to_broadcast([SMP, NB, P]),
                                       own_seq[:].unsqueeze(2).to_broadcast([SMP, NB, P]), ALU.mult), s_vb)

            def g_state(r):
                dve.wait_ge(s_ds, r + 1)
                if r:
                    dve.wait_ge(s_state_out, 32 * r)
                done(dve.tensor_copy(S[:, 0, :], A[2][:, 0:P]))
                for c in range(1, TT):
                    last = eb[:, (c + 1) * P - 1:(c + 1) * P]
                    done(dve.scalar_tensor_tensor(S[:, c, :], S[:, c - 1, :], last, A[2][:, c * P:(c + 1) * P], ALU.mult, ALU.add),
                         s_st if c == TT - 1 else None)

            def g_sample(r, h):
                dve.wait_ge(s_dss, 2 * r + h + 1)
                for b in range(4 * h, 4 * h + 4):
                    last = eb[:, SEQ + (b + 1) * NT - 1:SEQ + (b + 1) * NT]
                    if b == 0:
                        dve.wait_ge(s_s0, 16 * (r + 1))
                    done(dve.scalar_tensor_tensor(S1[:, b, :], S0[:, b, :], last, A[3 - h][:, (b % 4) * P:(b % 4 + 1) * P], ALU.mult, ALU.add),
                         s_sn if b % 4 == 3 else None)

            def g_scale(r):
                dve.wait_ge(s_rbo, r + 1)
                done(dve.scalar_tensor_tensor(orec[:, r, :], osc[:], vec[:, VN["hgrn"] + r:VN["hgrn"] + r + 1], rb[:], ALU.mult, ALU.mult), s_or)

            def y_put(k):
                dve.wait_ge(s_yt, k + 1)
                done(dve.tensor_copy(ysb[:, 0:TT, k * P:(k + 1) * P], A[1 + k % 2].rearrange("p (i c) -> p i c", c=P)), s_yc)
                done(dve.tensor_copy(ysb[0:SMP, TT, k * P:(k + 1) * P], A[3][0:SMP, 0:P]), s_yc)

            def final():
                dve.wait_ge(s_rbt, 2)
                for i in (0, 2, TT):
                    rows = P if i < TT else SMP
                    done(dve.tensor_scalar(ysb[0:rows, i, :], ysb[0:rows, i, :], rbt[0:rows, i:i + 1], None, ALU.mult), s_y[i])

            for ev, *x in walk():
                if ev == "front":
                    front()
                elif ev == "modulate":
                    modulate(*x)
                elif ev == "hi":
                    hi(*x)
                elif ev == "lo" and x[0] < 2 and x[1] == 0:
                    lo(x[0])
                elif ev == "ada_part":
                    ada_part(*x)
                elif ev == "evac":
                    evac(*x)
                elif ev == "finish_stats" and x[0] == 1:
                    for k in range(0, KT, 2):
                        scale_vectors(1, k)
                elif ev == "scan":
                    scan(*x)
                elif ev == "q_blocks":
                    q_blocks(*x)
                elif ev == "masks":
                    masks()
                elif ev == "a_max":
                    a_max(*x)
                elif ev == "a_scale":
                    a_scale(*x)
                elif ev == "win":
                    win()
                elif ev == "merge":
                    merge(*x)
                elif ev == "y_put":
                    y_put(*x)
                elif ev == "g_operands":
                    g_operands(*x)
                elif ev == "g_diag":
                    g_diag(*x)
                elif ev == "g_level":
                    g_level(*x)
                elif ev == "g_products":
                    g_products(*x)
                elif ev == "g_keys":
                    g_keys(*x)
                elif ev == "g_state":
                    g_state(*x)
                elif ev == "g_sample":
                    g_sample(*x)
                elif ev == "g_scale":
                    g_scale(*x)
                elif ev == "final":
                    final()

        @block.gpsimd
        def _(pool):
            done = ordered(pool, s_pool, {s_lo: 8})

            def lo(n, q):
                if n < 2:
                    return
                pool.wait_ge(s_hi, n + 1)
                w = wR[split_index(n)]
                cols = slice(q * UW // 4, (q + 1) * UW // 4)
                done(pool.tensor_tensor(w[:, 1, cols], raw[SLOT[SPLITS[n]]][:, cols], w[:, 0, cols].bitcast(F32), ALU.subtract), s_lo)

            def squares(n, k):
                if 0 < k <= SUMMED:
                    pool.wait_ge(s_sq, n * KT + k + 1)
                    done(pool.tensor_tensor(rb[:], rb[:], square(k)[:], ALU.add), s_acc)

            def modulate(n, k0):
                for k in (k0, k0 + 1):
                    pool.wait_ge(s_hhi, n * KT + k + 1)
                    cols = slice(k * TOK, (k + 1) * TOK)
                    done(pool.tensor_tensor(hR[:, 1, cols], tmp[k % 4][:], hR[:, 0, cols].bitcast(F32), ALU.subtract), s_hlo)

            def g_diff(r, l):
                m, n = LEVELS[l], r * NL + l
                if n == 0:
                    pool.wait_ge(s_score, STEPS + 1)
                if l == 0:
                    pool.wait_ge(s_scan, r + 1)
                if n >= 3:
                    pool.wait_ge(s_Kt, n - 2)
                w = TOK if m < NT else SEQ
                bv = B[r // 2 % 2][:, r % 2, 0:w].rearrange("p (a m) -> p a m", m=2 * m)
                done(pool.tensor_tensor(D[n % 3][:, 0:w].rearrange("p (a m) -> p a m", m=2 * m), bv,
                                        bv[:, :, m - 1:m].to_broadcast([P, w // (2 * m), 2 * m]), ALU.subtract), s_D)

            def g_hats(r):
                if r:
                    pool.wait_ge(s_or, r)
                for lo, hi, m, last in ((0, SEQ, P, False), (SEQ, TOK, NT, True)):
                    bv = B[r // 2 % 2][:, r % 2, lo:hi].rearrange("p (a m) -> p a m", m=m)
                    done(pool.tensor_tensor(kh[:, lo:hi].rearrange("p (a m) -> p a m", m=m), bv[:, :, m - 1:m].to_broadcast([P, (hi - lo) // m, m]),
                                            bv, ALU.subtract), s_dx if last else None)

            def g_products(r):
                pool.wait_ge(s_ex, r + 1)
                if r:
                    pool.wait_ge(s_out, r)
                else:
                    pool.wait_ge(s_win, (2 + 2 * NB) * 16)
                    pool.wait_ge(s_otc, STEPS - PREP)
                done(pool.tensor_tensor(qh[:], QS[r // 2 % 2][:, r % 2, :], eb[:], ALU.mult), s_qh)

            def evac(x):
                if x.kind == "up":
                    n = 2 * x.i + x.n
                    pool.wait_ge(s_ahi, n + 1)
                    a_ = actR[:, act_tile(x)]
                    done(pool.tensor_tensor(a_[:, 1, :], tmp[n % 2][:], a_[:, 0, :].bitcast(F32), ALU.subtract), s_alo)

            for ev, *x in walk():
                if ev == "lo":
                    lo(*x)
                elif ev == "norm":
                    for k in range(KT):
                        squares(0, k)
                elif ev == "stats":
                    squares(*x)
                elif ev == "modulate":
                    modulate(*x)
                elif ev == "g_diff":
                    g_diff(*x)
                elif ev == "g_hats":
                    g_hats(*x)
                elif ev == "g_products":
                    g_products(*x)
                elif ev == "evac":
                    evac(*x)


def constants():
    import numpy as np
    far = -1e30 * HD ** 0.5
    q, kk = np.arange(P)[:, None], np.arange(2 * P)[None]
    d = q + P - kk
    dist = np.stack([d, np.where((d >= 0) & (d <= WIN), 0.0, far)], 1).astype(np.float32)
    slope = (2.0 ** (-8.0 * np.arange(1, HEADS + 1) / HEADS))[np.arange(P) // NT][:, None]
    t = (np.arange(P) % NT)[:, None]
    dc = WIN + t - np.arange(P)[None]
    old = np.where((dc >= 0) & (dc <= WIN), -slope * dc * HD ** 0.5, far)
    i = np.arange(120)[None] - 56
    dn = t - i
    new = np.where((i >= 0) & (i < NT) & (dn >= 0), -slope * dn * HD ** 0.5, far)
    lv = np.zeros((P, NL, HALF), np.float32)
    s = np.arange(P)
    for l, m in enumerate(LEVELS):
        tt = np.arange(TOK).reshape(-1, 2 * m)[:, m:].ravel() if TOK % (2 * m) == 0 else np.arange(SEQ).reshape(-1, 2 * m)[:, m:].ravel()
        if m >= NT:
            tt = tt[tt < SEQ]
        for c, t_ in enumerate(tt):
            w = t_ % P
            lv[:, l, c] = (s // (2 * m) == w // (2 * m)) & (s % (2 * m) < m)
            if t_ >= SEQ:
                lv[SMP:, l, c] = 0
    resets = np.ones((P, TOK), np.float32)
    resets[:, 0:SEQ:P] = 0
    resets[:, SEQ::NT] = 0
    own = (np.arange(SMP)[:, None] // NT == np.arange(NB)[None]).astype(np.float32)
    return dict(k_ident=np.eye(P, dtype=np.float32), k_dist=dist.reshape(P, -1), k_bias_s=np.concatenate([old, new], 1).astype(np.float32),
                k_levels=lv.reshape(P, -1), k_resets=resets, k_own_seq=own)


_INS = ["x_prompt", "x_sample", "cache_win_k", "cache_win_v", "state_hgrn", "w_ada", "w_in", "attn_sinks", "w_out", "w_up", "w_down"]
_VECTORS = ["norm_mix", "norm_mlp", "hgrn_norm", "final_norm", "hgrn_lb_logits", "b_ada"]
_OUTS = dict(y_prompt=(1, SEQ, DM), y_sample=(NB, NT, DM), win_k_prompt=(1, 1, WIN, KV, HD), win_v_prompt=(1, 1, WIN, KV, HD),
             hgrn_prompt=(1, 1, RH, P, P), win_k_sample=(1, NB, WIN, KV, HD), win_v_sample=(1, NB, WIN, KV, HD),
             hgrn_sample=(1, NB, RH, P, P))


def kernel(**inputs):
    import numpy as np
    import concourse.bacc as bacc
    from concourse.bass_utils import run_bass_kernel_spmd

    nc = bacc.Bacc("TRN2", target_bir_lowering=False, num_devices=1, dynamic_dma_scratch_size=4096)
    given = {n: np.ascontiguousarray(inputs[n]) for n in _INS}
    given["c"] = np.concatenate([np.asarray(inputs["c_prompt"]), np.asarray(inputs["c_sample"])], 0)
    given["vectors"] = np.concatenate([np.asarray(inputs[n]).reshape(-1, P) for n in _VECTORS], 0)
    given["sink_rows"] = np.repeat(np.asarray(inputs["attn_sinks"])[0], NT)[:, None]
    given.update(constants())
    arrays, ins = {}, {}
    for name, v in given.items():
        arrays[f"in_{name}"] = v
        ins[name] = nc.dram_tensor(f"in_{name}", v.shape, mybir.dt.from_np(v.dtype), kind="ExternalInput").ap()
    outs = {n: nc.dram_tensor(f"out_{n}", s, F32, kind="ExternalOutput").ap() for n, s in _OUTS.items()}
    program(nc, ins, outs)
    r = run_bass_kernel_spmd(nc, [arrays], core_ids=[0])
    return tuple(r.results[0][f"out_{n}"] for n in _OUTS)
```
